# Optimizing a Trainium2 kernel written in Bass

```python
import jax, jax.numpy as jnp
from jax import lax
import numpy as np

D_MODEL = 1024
BATCH = 1
SEQ = 256
DEPTH = 1
DEC_BATCH = 8
DEC_SEQ = 8
PAST_LEN = 2048
PAGE_SIZE = 128

LRU_WIDTH = D_MODEL
LRU_HEADS = 16
LRU_BLOCK = LRU_WIDTH // LRU_HEADS
LRU_C = 8.0
CONV_A_WIDTH = 4
SC_WIDTH = D_MODEL
CONV_B_WIDTH = 3
IN_WIDTH = 2 * LRU_WIDTH + 3 * SC_WIDTH + 2 * D_MODEL
N_EXPERTS = 32
TOP_K = 4
D_FF = D_MODEL
SWIGLU_LIMIT = 7.0
SWIGLU_ALPHA = 1.702
MOE_BLOCK = 128
LN_EPS = 1e-5
DEEPNORM_ALPHA = (2.0 * DEPTH) ** 0.25
DEEPNORM_BETA = (8.0 * DEPTH) ** -0.25

kernel_name = "hawk_shortconv_moe_deepnorm_step"

def layernorm(x, g, b):
    xf = x.astype(jnp.float32)
    mu = jnp.mean(xf, axis=-1, keepdims=True)
    var = jnp.mean(jnp.square(xf - mu), axis=-1, keepdims=True)
    y = (xf - mu) * lax.rsqrt(var + LN_EPS) * g.astype(jnp.float32) + b.astype(jnp.float32)
    return y.astype(x.dtype)

def causal_dwconv(x, buf, w):
    width = w.shape[0]
    s = x.shape[1]
    xp = jnp.concatenate([buf.astype(x.dtype), x], axis=1)
    y = xp[:, 0:s] * w[0]
    for k in range(1, width):
        y = y + xp[:, k:k + s] * w[k]
    return y, xp[:, -(width - 1):]

def rglru(x, wa, ba, wx, bx, lam, h0):
    bsz, s, _ = x.shape
    xb = x.reshape(bsz, s, LRU_HEADS, LRU_BLOCK)
    r = jax.nn.sigmoid((jnp.einsum("bshi,hij->bshj", xb, wa).reshape(bsz, s, LRU_WIDTH) + ba).astype(jnp.float32))
    i = jax.nn.sigmoid((jnp.einsum("bshi,hij->bshj", xb, wx).reshape(bsz, s, LRU_WIDTH) + bx).astype(jnp.float32))
    log_a = -LRU_C * r * jax.nn.softplus(-lam.astype(jnp.float32))
    a = jnp.exp(log_a)
    b = jnp.sqrt(-jnp.expm1(2.0 * log_a)) * (i * x.astype(jnp.float32))
    b = b.at[:, 0].add(a[:, 0] * h0.astype(jnp.float32))

    def combine(left, right):
        a_l, b_l = left
        a_r, b_r = right
        return a_l * a_r, a_r * b_l + b_r

    _, h = lax.associative_scan(combine, (a, b), axis=1)
    return h.astype(x.dtype), h[:, -1].astype(x.dtype)

def moe_ffn(x, router_w, router_b, w_gu, b_gu, w_down, b_down):
    bsz, s, d = x.shape
    t = bsz * s
    x2 = x.reshape(t, d)
    logits = x2.astype(jnp.float32) @ router_w.astype(jnp.float32) + router_b.astype(jnp.float32)
    top_vals, top_idx = lax.top_k(logits, TOP_K)
    gates = jax.nn.softmax(top_vals, axis=-1).astype(x.dtype)
    n_assign = t * TOP_K
    flat_e = top_idx.reshape(n_assign).astype(jnp.int32)
    flat_tok = jnp.repeat(jnp.arange(t, dtype=jnp.int32), TOP_K)
    flat_w = gates.reshape(n_assign)
    order = jnp.argsort(flat_e)
    sorted_e = flat_e[order]
    counts = jnp.zeros((N_EXPERTS,), jnp.int32).at[flat_e].add(1)
    padded = (counts + MOE_BLOCK - 1) // MOE_BLOCK * MOE_BLOCK
    start = jnp.cumsum(counts) - counts
    end_pad = jnp.cumsum(padded)
    start_pad = end_pad - padded
    dest = start_pad[sorted_e] + jnp.arange(n_assign, dtype=jnp.int32) - start[sorted_e]
    n_blocks = -(-n_assign // MOE_BLOCK) + N_EXPERTS
    n_rows = n_blocks * MOE_BLOCK
    row_tok = jnp.full((n_rows,), t, jnp.int32).at[dest].set(flat_tok[order])
    row_w = jnp.zeros((n_rows,), x.dtype).at[dest].set(flat_w[order])
    block_e = jnp.minimum(
        jnp.searchsorted(end_pad, jnp.arange(n_blocks, dtype=jnp.int32) * MOE_BLOCK, side="right"),
        N_EXPERTS - 1)
    x_rows = jnp.concatenate([x2, jnp.zeros((1, d), x.dtype)], axis=0)[row_tok]
    x_rows = x_rows.reshape(n_blocks, MOE_BLOCK, d)

    def expert_block(args):
        xb, e = args
        gu = xb @ w_gu[e] + b_gu[e]
        gate = jnp.minimum(gu[:, :D_FF], SWIGLU_LIMIT)
        up = jnp.clip(gu[:, D_FF:], -SWIGLU_LIMIT, SWIGLU_LIMIT)
        h = (up + 1.0) * (gate * jax.nn.sigmoid(SWIGLU_ALPHA * gate))
        return h @ w_down[e] + b_down[e]

    y_rows = lax.map(expert_block, (x_rows, block_e)).reshape(n_rows, d)
    y = jax.ops.segment_sum(y_rows * row_w[:, None], row_tok, num_segments=t + 1)[:t]
    return y.reshape(bsz, s, d)

def hybrid_layer(x, h0, conv_a_buf, sc_buf, w_in, b_in, conv_a_w, conv_a_b, lru_wa, lru_ba, lru_wx, lru_bx,
                 lru_lambda, conv_b_w, w_out, ln1_g, ln1_b, router_w, router_b, w_gu, b_gu, w_down, b_down,
                 ln2_g, ln2_b):
    proj = x @ w_in + b_in
    splits = [LRU_WIDTH, 2 * LRU_WIDTH, 2 * LRU_WIDTH + SC_WIDTH, 2 * LRU_WIDTH + 2 * SC_WIDTH,
              2 * LRU_WIDTH + 3 * SC_WIDTH, 2 * LRU_WIDTH + 3 * SC_WIDTH + D_MODEL]
    xa, ga, b_gate, c_gate, v_sc, m_a, m_b = jnp.split(proj, splits, axis=-1)
    xa_c, conv_a_new = causal_dwconv(xa, conv_a_buf, conv_a_w)
    h, h_last = rglru(xa_c + conv_a_b, lru_wa, lru_ba, lru_wx, lru_bx, lru_lambda, h0)
    y_a = h * jax.nn.gelu(ga)
    u_c, sc_new = causal_dwconv(c_gate * v_sc, sc_buf, conv_b_w)
    y_b = b_gate * u_c
    mixed = (jax.nn.sigmoid(m_a) * y_a + jax.nn.sigmoid(m_b) * y_b) @ w_out
    x = layernorm(DEEPNORM_ALPHA * x + mixed, ln1_g, ln1_b)
    x = layernorm(DEEPNORM_ALPHA * x + moe_ffn(x, router_w, router_b, w_gu, b_gu, w_down, b_down), ln2_g, ln2_b)
    return x, h_last, conv_a_new, sc_new

def setup_inputs(seed: int = 0) -> dict:
    key = jax.random.key(seed)
    ks = jax.random.split(key, 26)
    nrm = lambda k, shape, scale: scale * jax.random.normal(k, shape, jnp.float32)
    u = jax.random.uniform(ks[9], (DEPTH, LRU_WIDTH), jnp.float32, 0.9, 0.999)
    a0 = u ** (1.0 / LRU_C)
    lru_lambda = jnp.log(a0) - jnp.log1p(-a0)
    return {
        "x_prompt": nrm(ks[0], (BATCH, SEQ, D_MODEL), 1.0),
        "x_sample": nrm(ks[1], (DEC_BATCH, DEC_SEQ, D_MODEL), 1.0),
        "state_rglru_h": nrm(ks[2], (DEPTH, DEC_BATCH, LRU_WIDTH), 0.5),
        "state_rglru_conv": nrm(ks[3], (DEPTH, DEC_BATCH, CONV_A_WIDTH - 1, LRU_WIDTH), 1.0),
        "state_shortconv": nrm(ks[4], (DEPTH, DEC_BATCH, CONV_B_WIDTH - 1, SC_WIDTH), 1.0),
        "w_in": nrm(ks[5], (DEPTH, D_MODEL, IN_WIDTH), D_MODEL ** -0.5),
        "b_in": nrm(ks[6], (DEPTH, IN_WIDTH), 0.02),
        "conv_a_w": nrm(ks[7], (DEPTH, CONV_A_WIDTH, LRU_WIDTH), CONV_A_WIDTH ** -0.5),
        "conv_a_b": nrm(ks[8], (DEPTH, LRU_WIDTH), 0.02),
        "lru_wa": nrm(ks[10], (DEPTH, LRU_HEADS, LRU_BLOCK, LRU_BLOCK), LRU_BLOCK ** -0.5),
        "lru_ba": nrm(ks[11], (DEPTH, LRU_WIDTH), 0.02),
        "lru_wx": nrm(ks[12], (DEPTH, LRU_HEADS, LRU_BLOCK, LRU_BLOCK), LRU_BLOCK ** -0.5),
        "lru_bx": nrm(ks[13], (DEPTH, LRU_WIDTH), 0.02),
        "lru_lambda": lru_lambda,
        "conv_b_w": nrm(ks[14], (DEPTH, CONV_B_WIDTH, SC_WIDTH), CONV_B_WIDTH ** -0.5),
        "w_out": nrm(ks[15], (DEPTH, D_MODEL, D_MODEL), DEEPNORM_BETA * D_MODEL ** -0.5),
        "ln1_g": 1.0 + nrm(ks[16], (DEPTH, D_MODEL), 0.02),
        "ln1_b": nrm(ks[17], (DEPTH, D_MODEL), 0.02),
        "router_w": nrm(ks[18], (DEPTH, D_MODEL, N_EXPERTS), D_MODEL ** -0.5),
        "router_b": nrm(ks[19], (DEPTH, N_EXPERTS), 0.01),
        "w_gu": nrm(ks[20], (DEPTH, N_EXPERTS, D_MODEL, 2 * D_FF), D_MODEL ** -0.5),
        "b_gu": nrm(ks[21], (DEPTH, N_EXPERTS, 2 * D_FF), 0.02),
        "w_down": nrm(ks[22], (DEPTH, N_EXPERTS, D_FF, D_MODEL), DEEPNORM_BETA * D_FF ** -0.5),
        "b_down": nrm(ks[23], (DEPTH, N_EXPERTS, D_MODEL), 0.02),
        "ln2_g": 1.0 + nrm(ks[24], (DEPTH, D_MODEL), 0.02),
        "ln2_b": nrm(ks[25], (DEPTH, D_MODEL), 0.02),
    }

def reference(x_prompt, x_sample, state_rglru_h, state_rglru_conv, state_shortconv, w_in, b_in, conv_a_w,
              conv_a_b, lru_wa, lru_ba, lru_wx, lru_bx, lru_lambda, conv_b_w, w_out, ln1_g, ln1_b, router_w,
              router_b, w_gu, b_gu, w_down, b_down, ln2_g, ln2_b):
    xp, xs = x_prompt, x_sample
    bp = x_prompt.shape[0]
    hp_l, cp_l, sp_l, hs_l, cs_l, ss_l = [], [], [], [], [], []
    for l in range(DEPTH):
        params = (w_in[l], b_in[l], conv_a_w[l], conv_a_b[l], lru_wa[l], lru_ba[l], lru_wx[l], lru_bx[l],
                  lru_lambda[l], conv_b_w[l], w_out[l], ln1_g[l], ln1_b[l], router_w[l], router_b[l],
                  w_gu[l], b_gu[l], w_down[l], b_down[l], ln2_g[l], ln2_b[l])
        h0 = jnp.zeros((bp, LRU_WIDTH), xp.dtype)
        ca0 = jnp.zeros((bp, CONV_A_WIDTH - 1, LRU_WIDTH), xp.dtype)
        cb0 = jnp.zeros((bp, CONV_B_WIDTH - 1, SC_WIDTH), xp.dtype)
        xp, hp, cp, sp = hybrid_layer(xp, h0, ca0, cb0, *params)
        xs, hs, cs, ss = hybrid_layer(xs, state_rglru_h[l], state_rglru_conv[l], state_shortconv[l], *params)
        hp_l.append(hp); cp_l.append(cp); sp_l.append(sp)
        hs_l.append(hs); cs_l.append(cs); ss_l.append(ss)
    return (xp, xs, jnp.stack(hp_l), jnp.stack(cp_l), jnp.stack(sp_l), jnp.stack(hs_l), jnp.stack(cs_l),
            jnp.stack(ss_l))


_drawn_inputs = setup_inputs


def setup_inputs(seed=0):
    import zlib

    import numpy as np

    out = dict(_drawn_inputs(seed))
    spreads = {}
    factors = {'lru_ba': 8.0,
     'lru_bx': 7.129,
     'router_b': 3.084,
     'b_gu': 8.0,
     'b_down': 6.379,
     'ln2_g': 2.85,
     'ln2_b': 2.807}
    for name, (base, spread) in spreads.items():
        noise = np.random.default_rng([zlib.crc32(name.encode()), seed]).standard_normal(out[name].shape)
        drawn = base * np.exp(spread * noise) if base else spread * noise
        out[name] = __import__('jax').numpy.asarray(drawn.astype(out[name].dtype))
    for name, factor in factors.items():
        out[name] = (out[name] * factor).astype(out[name].dtype)
    return out
```

```python
from contextlib import ExitStack

import concourse.bass as bass
from concourse import mybir

P = 128
D = 1024
KC = D // P
SEQ, DB, DS = 256, 8, 8
NS = DB * DS
T = SEQ + NS
TILES = [(0, P), (P, P), (2 * P, NS)]
IN_W = 7 * D
GW = 256
NG = D // GW
SPG = GW // P
NE, TOPK, FF = 32, 4, 1024
ROWS = 64
MAX_EXTRA = T * TOPK // ROWS
NB = (T + ROWS - 1) // ROWS
HALF = 512
ALPHA = 2.0 ** 0.25
EPS = 1e-5
LIMIT, SW_ALPHA = 7.0, 1.702

XA, GA, BG, CG, V, MA, MB = range(7)
ORDER = [XA, CG, V, GA, BG, MA, MB]
CAW, CAB, LBA, LBX, LAM, CBW, BIN = 0, 32, 40, 48, 56, 64, 88
NPRM = BIN + 7 * KC

ALU = mybir.AluOpType
ACT = mybir.ActivationFunctionType
AX_X = mybir.AxisListType.X
F32 = mybir.dt.float32
I32 = mybir.dt.int32
U32 = mybir.dt.uint32
ds = bass.ds


XB, TB, CB = 2, 3, (4, 6, 4)
K_DENSE, K_PAIR = 40, 4


class Chain:

    def __init__(self, eng, sem):
        self.eng, self.sem, self.n, self.off = eng, sem, 0, 0

    def __call__(self, ins):
        ins.then_inc(self.sem, 1)
        self.n += 1
        self.eng.wait_ge(self.sem, self.off + self.n)


def hybrid_layer(nc, x_prompt, x_sample, state_h, state_conv, state_sc, w_in, b_in, conv_a_w,
                 conv_a_b, lru_wa, lru_ba, lru_wx, lru_bx, lru_lambda, conv_b_w, w_out, ln1_g,
                 ln1_b, router_w, router_b, w_gu, b_gu, w_down, b_down, ln2_g, ln2_b,
                 y_prompt, y_sample, h_prompt, conv_prompt, sc_prompt, h_sample, conv_sample,
                 sc_sample):
    ctx = ExitStack()
    with ctx:
        def sb(name, shape, dt=F32):
            return ctx.enter_context(nc.sbuf_tensor(name, shape, dt))

        def sem(name):
            return ctx.enter_context(nc.semaphore(name))

        ring_gu = sb("ring_gu", [P, 8, 2 * FF])
        ring_dn = sb("ring_dn", [P, 8, 2 * D])
        x_tok = sb("x_tok", [P, 3, D])
        x1 = sb("x1", [P, 3, D])
        y_acc = x_tok
        wab = x1[:, 0:2, :].rearrange("p a (c n) -> p a c n", c=KC)
        st_rows = x1[:, 2, :]
        xT = sb("xT", [P, KC, T])
        mixT = sb("mixT", [P, KC, T])
        bgu = mixT[:, :, :].rearrange("p k t -> p (k t)")[0:NE, 0:2 * FF]
        bdn = sb("bdn", [NE, D])
        scratch = sb("scratch", [P, 14 * 360])
        so_rows = scratch[0:54, 1536:1536 + D]
        vrows = sb("vrows", [P, 2, P])
        prm = sb("prm", [P, NPRM])
        bhalf = sb("bhalf", [P, 2 * KC])
        ghalf = sb("ghalf", [P, 2 * KC])
        sp2 = sb("sp2", [P, KC])
        spt = sb("spt", [P, 4, KC])
        stT = sb("stT", [P, KC, 48])
        so = sb("so", [P, KC, 54])
        wcur = sb("wcur", [P, 2, P])
        ident = sb("ident", [P, P])
        upper = sb("upper", [P, P])
        ones = sb("ones", [P, P])
        iota = sb("iota", [P, (NB + 1) * ROWS])
        rw = sb("rw", [P, KC, NE])
        rb = sb("rb", [P, NE])
        posm = sb("posm", [P, 3, NE])
        gate = sb("gate", [P, 3, NE])
        gateh = sb("gateh", [P, 3, NE])
        items = sb("items", [1, 2, 64], I32)
        pairs = sb("pairs", [1, 4], I32)
        stat = sb("stat", [P, 3, 2, 6])
        mv = sb("mv", [P, 3, 8])
        small = sb("small", [P, 8])

        PS = ctx.enter_context(nc.psum_tensor("PS", [P, 8, HALF], F32))

        W = 360

        def dense(i, n=T):
            return scratch[:, i * W:i * W + n]
        xa_pad, cv_pad, gel, bgt, cgt, vt, tma, tmb, xc, tr, ti, rr, aa, sq = (
            dense(i, n) for i, n in enumerate([347, 338] + [T] * 12))
        hh = vt
        uc = cgt
        xa_p, xa_s = xa_pad[:, 0:259], xa_pad[:, 259:347].rearrange("p (b s) -> p b s", b=DB)
        cv_p, cv_s = cv_pad[:, 0:258], cv_pad[:, 258:338].rearrange("p (b s) -> p b s", b=DB)

        def pr(t):
            return t[:, 0:SEQ]

        def sm(t):
            return t[:, SEQ:T].rearrange("p (b s) -> p b s", b=DB)

        def half(i):
            return scratch[:, i * HALF:(i + 1) * HALF]
        gm, th, up, y_sb, xg_sb, xgT_f, hT_f = (half(i) for i in range(7))
        xgT = xgT_f.rearrange("p (j a r) -> p j a r", j=4, a=2)
        hT = hT_f.rearrange("p (j a r) -> p j a r", j=4, a=2)
        free = 7 * HALF
        xTf = xT[:, :, :].rearrange("p k t -> p (k t)")
        onehot = xTf[:, 0:3 * ROWS].rearrange("p (t r) -> p t r", t=3)
        cgate = xTf[:, 192:192 + 3 * P].rearrange("p (t a r) -> p t a r", t=3, a=2)
        gt_sb = xTf[:, 576:576 + 2 * T].rearrange("p (s t) -> p s t", s=2)
        esel = xTf[0:NE, 1216:1216 + 2 * ROWS].rearrange("p (s r) -> p s r", s=2)
        gT = xTf[0:NE, 1600:1600 + T]
        at = [free]

        def route(n):
            at[0] += n
            return scratch[:, at[0] - n:at[0]]
        lg = route(96).rearrange("p (t e) -> p t e", t=3)
        mask = route(96).rearrange("p (t e) -> p t e", t=3)
        cnt, ext, incl, excl = (route(32) for _ in range(4))
        top = route(24).rearrange("p (t k) -> p t k", t=3)
        idx = route(24).bitcast(U32).rearrange("p (t k) -> p t k", t=3)
        idf = route(24).rearrange("p (t k) -> p t k", t=3)
        ek = route(12).rearrange("p (t k) -> p t k", t=3)
        es = route(3)
        tabf = route(128).rearrange("p (a q) -> p a q", a=2)
        prf = route(12)
        assert at[0] <= 14 * W
        oh4 = scratch[:, 0:384].rearrange("p (t k e) -> p t k e", t=3, k=TOPK)
        og4 = scratch[:, 512:896].rearrange("p (t k e) -> p t k e", t=3, k=TOPK)
        tb0 = scratch[0:1, 0:22 * NE].rearrange("p (q e) -> p q e", q=22)
        tb1 = scratch[0:1, 768:768 + 22 * NE].rearrange("p (q e) -> p q e", q=22)

        x_in = sem("x_in")
        prm_in, st_in, wab_in, misc_in, ln_in = (sem(n) for n in
                                                 ("prm_in", "st_in", "wab_in", "misc_in", "ln_in"))
        win_in = [sem(f"win_in{j}") for j in range(7)]
        wout_in = [sem(f"wout_in{j}") for j in range(4)]
        bias_in = sem("bias_in")
        ln2_in = sem("ln2_in")
        gu_in = [sem(f"gu_in{k}") for k in range(8)]
        dn_in = [sem(f"dn_in{k}") for k in range(8)]
        const_ok, zero_ok, pool_own = sem("const_ok"), sem("zero_ok"), sem("pool_own")
        x_turned, prm_turned, st_turned = sem("x_turned"), sem("prm_turned"), sem("st_turned")
        proj_done, proj_taken = sem("proj_done"), sem("proj_taken")
        gates_done, gates_taken = sem("gates_done"), sem("gates_taken")
        wcur_ok = sem("wcur_ok")
        prm_ok = sem("prm_ok")
        xa_free, cv_free, xc_ok, block_ok = sem("xa_free"), sem("cv_free"), sem("xc_ok"), sem("block_ok")
        t_ok, sq_ok = sem("t_ok"), sem("sq_ok")
        wout_done, r_taken = sem("wout_done"), sem("r_taken")
        so_turned, so_ok = sem("so_turned"), sem("so_ok")
        var_ok, std_ok, x1_ok = sem("var_ok"), sem("std_ok"), sem("x1_ok")
        x1_turned, x1T_ok, lg_done, lg_taken = (sem(n) for n in ("x1_turned", "x1T_ok", "lg_done", "lg_taken"))
        top_ok, exp_ok = sem("top_ok"), sem("exp_ok")
        mask_ok, rank_done, gate_ok = sem("mask_ok"), sem("rank_done"), sem("gate_ok")
        g_turned, gT_ok = sem("g_turned"), sem("gT_ok")
        items_ok = sem("items_ok")
        oh_ok, cg_ok = sem("oh_ok"), sem("cg_ok")
        xg_done, xg_ok, tx_done, xgT_ok = (sem(n) for n in ("xg_done", "xg_ok", "tx_done", "xgT_ok"))
        gt_done, gt_ok = sem("gt_done"), sem("gt_ok")
        gu_used, dn_used = sem("gu_used"), sem("dn_used")
        gm_ok, th_ok, h_ok, ht_done, hT_ok, y_ok = (
            sem(n) for n in ("gm_ok", "th_ok", "h_ok", "ht_done", "hT_ok", "y_ok"))
        c_done, c_taken = sem("c_done"), sem("c_taken")
        out_ok, out_sem, so_out = sem("out_ok"), sem("out_sem"), sem("so_out")
        dve_own, dve_end = sem("dve_own"), sem("dve_end")

        block = ctx.enter_context(nc.Block())

        win_v = w_in[0].rearrange("(k p) n -> p k n", p=P)
        wout_v = w_out[0].rearrange("(k p) n -> p k n", p=P)
        slot_in = ring_dn[:, 0:7, :].rearrange("p j (k n) -> p j k n", k=KC)
        slot_out = ring_dn[:, 0:4, :].rearrange("p j (k n) -> p j k n", k=2)
        ln_g, ln_b = ring_dn[:, 7, 0:D], ring_dn[:, 7, D:2 * D]

        @block.sync
        def _(sp):
            sp.dma_start(x_tok[:, 0:2, :], x_prompt[0].rearrange("(t p) d -> p t d", p=P)).then_inc(x_in, 16)
            sp.dma_start(x_tok[0:NS, 2, :], x_sample.rearrange("b s d -> (b s) d")).then_inc(x_in, 16)

            def load_in(g, j):
                sp.dma_start(slot_in[:, j], win_v[:, :, ds(g * GW + ORDER[j] * D, GW)]).then_inc(win_in[j], 16)

            for j in range(7):
                load_in(0, j)
            for k in range(8):
                sp.dma_start(ring_gu[:, k], w_gu[0, 0, k * P:(k + 1) * P, :]).then_inc(gu_in[k], 16)
            with sp.Fori(1, NG) as g:
                for j in range(7):
                    sp.wait_ge(proj_done, g * (7 * SPG) + (j - 6))
                    load_in(g, j)
            for j in range(4):
                sp.wait_ge(proj_done, 7 * (SPG * NG - 1) + j + 1)
                sp.dma_start(slot_out[:, j], wout_v[:, 2 * j:2 * j + 2, :]).then_inc(wout_in[j], 16)
            sp.wait_ge(wout_done, 3)
            sp.dma_start(bgu, b_gu[0]).then_inc(bias_in, 16)
            sp.dma_start(bdn[:, :], b_down[0]).then_inc(bias_in, 16)

            def load_gu(e, k):
                sp.dma_start(ring_gu[:, k], w_gu[0, ds(e, 1), k * P:(k + 1) * P, :]
                             .rearrange("a p n -> p (a n)")).then_inc(gu_in[k], 16)

            def load_dn(e, s, u):
                sp.dma_start(ring_dn[:, 4 * s + u, :].rearrange("p (k n) -> p k n", k=2),
                             w_down[0, ds(e, 1), 2 * u * P:(2 * u + 2) * P, :]
                             .rearrange("a (k p) n -> p (a k) n", p=P)).then_inc(dn_in[4 * s + u], 16)

            for s in range(2):
                for u in range(4):
                    if s == 1 and u == 3:
                        sp.wait_ge(x1_ok, 3)
                    load_dn(s, s, u)
            for k in range(8):
                sp.wait_ge(gu_used, k + 1)
                load_gu(1, k)

            def load_pair(p, experts):
                for s in range(2):
                    for k in range(8):
                        sp.wait_ge(gu_used, 16 * p + (8 * s + k - 7))
                        load_gu(experts[s], k)
                    for u in range(4):
                        sp.wait_ge(dn_used, 8 * p + (4 * s + u - 7))
                        load_dn(experts[s], s, u)

            with sp.Fori(1, NE // 2) as p:
                load_pair(p, [2 * p, 2 * p + 1])
            sp.wait_ge(items_ok, 1)
            n_pairs = sp.value_load(pairs[0:1, 0:1], min_val=NE // 2, max_val=(NE + MAX_EXTRA) // 2)
            with sp.If(n_pairs > NE // 2):
                with sp.Fori(NE // 2, n_pairs) as p:
                    ea = sp.value_load(items[0:1, 0, ds(2 * p, 1)], min_val=0, max_val=NE - 1)
                    eb = sp.value_load(items[0:1, 0, ds(2 * p + 1, 1)], min_val=0, max_val=NE - 1)
                    load_pair(p, [ea, eb])
            sp.wait_ge(dn_used, 8 * n_pairs)
            sp.dma_start(ln_g, ln2_g[0:1, :].to_broadcast([P, D])).then_inc(ln2_in, 16)
            sp.dma_start(ln_b, ln2_b[0:1, :].to_broadcast([P, D])).then_inc(ln2_in, 16)
            for q, t in enumerate((1, 2, 0)):
                t0, n = TILES[t]
                sp.wait_ge(out_ok, q + 1)
                dst = y_prompt[0, t0:t0 + n, :] if t < 2 else y_sample.rearrange("b s d -> (b s) d")
                sp.dma_start(dst, x1[0:n, t, :]).then_inc(out_sem, 16)
            sp.wait_ge(out_sem, 48)

        @block.gpsimd
        def _(pool):
            pool.memset(ident[:, :], 0.0).then_inc(pool_own, 1)
            pool.memset(upper[:, :], 1.0).then_inc(pool_own, 1)
            pool.memset(ones[:, :], 1.0).then_inc(const_ok, 1)
            pool.wait_ge(pool_own, 2)
            pool.affine_select(out=ident[:, :], in_=ident[:, :], compare_op=ALU.not_equal, fill=1.0,
                               base=0, pattern=[[-1, P]], channel_multiplier=1).then_inc(const_ok, 1)
            pool.affine_select(out=upper[:, :], in_=upper[:, :], compare_op=ALU.is_gt, fill=0.0,
                               base=0, pattern=[[1, P]], channel_multiplier=-1).then_inc(const_ok, 1)
            pool.memset(wab, 0.0).then_inc(zero_ok, 1)
            pool.iota(iota[:, :], pattern=[[1, (NB + 1) * ROWS]], base=0, channel_multiplier=0,
                      allow_small_or_imprecise_dtypes=True).then_inc(const_ok, 1)
            pool.wait_ge(wab_in, 64)
            pool.tensor_copy(wcur[:, :, :], wab[:, :, 0, :]).then_inc(wcur_ok, 1)
            with pool.Fori(1, KC) as c:
                pool.wait_ge(gates_done, 2 * c)
                pool.tensor_copy(wcur[:, 0, :], wab[:, 0, ds(c, 1), :].rearrange("p a n -> p (a n)"))
                pool.tensor_copy(wcur[:, 1, :], wab[:, 1, ds(c, 1), :].rearrange("p a n -> p (a n)")).then_inc(wcur_ok, 1)

        @block.scalar
        def _(act):
            rows = 0
            for src, n in ((conv_a_w, 32), (conv_a_b, 8), (lru_ba, 8), (lru_bx, 8), (lru_lambda, 8), (conv_b_w, 24)):
                v = src[0] if n > 8 else src
                act.dma_start(vrows[rows:rows + n, 0, :], v.rearrange("a (c p) -> (a c) p", p=P)).then_inc(prm_in, 16)
                rows += n
            act.dma_start(vrows[0:7 * KC, 1, :], b_in.rearrange("a (c p) -> (a c) p", p=P)).then_inc(prm_in, 16)
            act.dma_start(st_rows[0:8, :], state_h[0]).then_inc(st_in, 16)
            act.dma_start(st_rows[8:32, :], state_conv[0].rearrange("b j d -> (b j) d")).then_inc(st_in, 16)
            act.dma_start(st_rows[32:48, :], state_sc[0].rearrange("b j d -> (b j) d")).then_inc(st_in, 16)
            act.wait_ge(zero_ok, 1)
            for a, w in enumerate((lru_wa, lru_wx)):
                for j in range(2):
                    act.dma_start(wab[64 * j:64 * j + 64, a, :, 64 * j:64 * j + 64],
                                  w[0].rearrange("(c j) i o -> j i c o", j=2)[j]).then_inc(wab_in, 16)
            act.dma_start(rw[:, :, :], router_w[0].rearrange("(k p) e -> p k e", p=P)).then_inc(misc_in, 16)
            act.dma_start(rb[:, :], router_b[0:1, :].to_broadcast([P, NE])).then_inc(misc_in, 16)
            act.dma_start(ln_g, ln1_g[0:1, :].to_broadcast([P, D])).then_inc(ln_in, 16)
            act.dma_start(ln_b, ln1_b[0:1, :].to_broadcast([P, D])).then_inc(ln_in, 16)

            for k in range(KC):
                act.wait_ge(x_turned, k + 1)
                act.activation(xT[:, k, :], PS[:, k % 6, 0:T], ACT.Copy).then_inc(proj_taken, 1)
            act.wait_ge(prm_turned, 1)
            act.activation(prm[:, :], PS[:, 6, 0:NPRM], ACT.Copy).then_inc(gates_taken, 1)
            act.wait_ge(st_turned, 1)
            act.activation(stT[:, :, :], PS[:, 7, 0:KC * 48].rearrange("p (k r) -> p k r", k=KC), ACT.Copy)\
               .then_inc(gates_taken, 1)
            act.wait_ge(prm_ok, 1)
            act.activation(spt[:, 0, :], spt[:, 1, :], ACT.Exp, scale=-1.0).then_inc(prm_ok, 1)
            act.wait_ge(prm_ok, 3)

            def bias(m, c):
                return prm[:, ds(c + (BIN + m * KC), 1)]

            with act.Fori(0, NG) as g:
                for s in range(SPG):
                    c = g * SPG + s
                    for j, m in enumerate(ORDER):
                        act.wait_ge(proj_done, g * (7 * SPG) + (7 * s + j + 1))
                        ps = PS[:, j % 6, 0:T]
                        if m == XA:
                            act.wait_ge(xa_free, g * SPG + (s + 1))
                            act.activation(xa_p[:, 3:259], pr(ps), ACT.Identity, bias=bias(m, c))
                            act.activation(xa_s[:, :, 3:11], sm(ps), ACT.Identity, bias=bias(m, c))\
                               .then_inc(proj_taken, 1)
                            continue
                        if m == CG:
                            act.wait_ge(block_ok, g * SPG + (s + 1))
                        if m in (CG, V, BG):
                            dst = {CG: cgt, V: vt, BG: bgt}[m]
                            act.activation(dst, ps, ACT.Identity, bias=bias(m, c)).then_inc(proj_taken, 1)
                        elif m == GA:
                            act.activation(gel, ps, ACT.Gelu_apprx_tanh, bias=bias(m, c)).then_inc(proj_taken, 1)
                        else:
                            dst, o = (tma, 0) if m == MA else (tmb, KC)
                            act.activation(dst, ps, ACT.Tanh, bias=bhalf[:, ds(c + o, 1)], scale=0.5)\
                               .then_inc(proj_taken, 1)
                    act.wait_ge(gates_done, g * (2 * SPG) + (2 * s + 2))
                    act.activation(ti, PS[:, 7, 0:T], ACT.Tanh, bias=ghalf[:, ds(c + KC, 1)], scale=0.5)\
                       .then_inc(gates_taken, 1)
                    act.activation(tr, PS[:, 6, 0:T], ACT.Tanh, bias=ghalf[:, ds(c, 1)], scale=0.5)\
                       .then_inc(gates_taken, 1)
                    act.wait_ge(gates_taken, g * (2 * SPG) + (2 * s + 4))
                    act.activation(tr, tr, ACT.Tanh, bias=sp2[:, ds(c, 1)], scale=sp2[:, ds(c, 1)])\
                       .then_inc(t_ok, 1)
                    act.wait_ge(t_ok, g * SPG + (s + 1))
                    act.activation(sq, tr, ACT.Sqrt).then_inc(sq_ok, 1)

            for t, (t0, n) in enumerate(TILES):
                act.wait_ge(var_ok, t + 1)
                act.activation(mv[0:n, t, 3:4], mv[0:n, t, 2:3], ACT.Sqrt).then_inc(std_ok, 1)
            act.wait_ge(so_turned, 1)
            act.activation(so_rows.rearrange("r (a n) -> r a n", a=2), PS[0:54, 6:8, :], ACT.Copy)\
               .then_inc(so_ok, 1)
            act.wait_ge(so_ok, 1)
            row = 0
            for dst, n in ((h_prompt[0], 1), (h_sample[0], 8), (conv_prompt[0, 0], 3),
                           (conv_sample[0].rearrange("b j d -> (b j) d"), 24), (sc_prompt[0, 0], 2),
                           (sc_sample[0].rearrange("b j d -> (b j) d"), 16)):
                act.dma_start(dst, so_rows[row:row + n, :]).then_inc(so_out, 16)
                row += n
            for t, (t0, n) in enumerate(TILES):
                act.wait_ge(x1_turned, t + 1)
                b = (6, 0, 2)[t]
                act.activation(xT[:, :, t0:t0 + n],
                               PS[:, b:b + 2, :].rearrange("p a (k m) -> p (a k) m", m=P)[:, :, 0:n], ACT.Copy)\
                   .then_inc(x1T_ok, 1)
            act.wait_ge(top_ok, 1)
            act.activation(ek, ek, ACT.Exp).then_inc(exp_ok, 1)
            act.wait_ge(g_turned, 1)
            act.activation(gT, PS[0:NE, 6, 0:T], ACT.Copy).then_inc(gT_ok, 1)

            def take_xg(count):
                act.wait_ge(xg_done, count)
                act.activation(xg_sb, PS[:, XB, :], ACT.Copy).then_inc(xg_ok, 1)

            def take_xgT(count):
                act.wait_ge(tx_done, count)
                act.activation(xgT_f, PS[:, TB, :], ACT.Copy).then_inc(xgT_ok, 1)

            take_xg(1)
            take_xgT(1)
            act.wait_ge(items_ok, 1)
            n_pairs = act.value_load(pairs[0:1, 0:1], min_val=NE // 2, max_val=(NE + MAX_EXTRA) // 2)
            with act.Fori(0, n_pairs) as p:
                for s in range(2):
                    act.wait_ge(gm_ok, p * 2 + (s + 1))
                    act.activation(th, gm, ACT.Tanh, scale=SW_ALPHA / 2).then_inc(th_ok, 1)
                    take_xg(p * 2 + (s + 2))
                    act.wait_ge(gt_done, p * 2 + (s + 1))
                    act.activation(gt_sb[:, s, :], PS[:, TB, 0:T], ACT.Copy).then_inc(gt_ok, 1)
                    take_xgT(p * 2 + (s + 2))
                    act.wait_ge(ht_done, p * 2 + (s + 1))
                    act.activation(hT_f, PS[:, TB, :], ACT.Copy).then_inc(hT_ok, 1)
                    act.wait_ge(dn_used, p * 8 + (4 * s + 4))
                    act.activation(y_sb, PS[:, XB, :], ACT.Copy).then_inc(y_ok, 1)
            for q, t in enumerate((1, 2, 0)):
                n = TILES[t][1]
                act.wait_ge(var_ok, q + 4)
                act.activation(mv[0:n, t, 3:4], mv[0:n, t, 2:3], ACT.Sqrt).then_inc(std_ok, 1)
            act.wait_ge(so_out, 96)

        @block.tensor
        def _(pe):
            mm = pe.matmul
            pe.wait_ge(const_ok, 4)
            pe.wait_ge(x_in, 32)
            for k in range(KC):
                if k >= 6:
                    pe.wait_ge(proj_taken, k - 5)
                for t, (t0, n) in enumerate(TILES):
                    last = pe.transpose(PS[:, k % 6, t0:t0 + n], x_tok[0:n, t, k * P:(k + 1) * P], ident[0:n, 0:n])
                last.then_inc(x_turned, 1)
            pe.wait_ge(prm_in, 112)
            pe.transpose(PS[:, 6, 0:BIN], vrows[0:BIN, 0, :], ident[0:BIN, 0:BIN])
            pe.transpose(PS[:, 6, BIN:NPRM], vrows[0:7 * KC, 1, :], ident[0:7 * KC, 0:7 * KC]).then_inc(prm_turned, 1)
            pe.wait_ge(st_in, 48)
            for k in range(KC):
                last = pe.transpose(PS[:, 7, k * 48:(k + 1) * 48], st_rows[0:48, k * P:(k + 1) * P], ident[0:48, 0:48])
            last.then_inc(st_turned, 1)
            pe.wait_ge(proj_taken, KC)

            with pe.Fori(0, NG) as g:
                for s in range(SPG):
                    for j in range(7):
                        if s == 0:
                            pe.wait_ge(win_in[j], g * 16 + 16)
                        pe.wait_ge(proj_taken, g * (7 * SPG) + (7 * s + {0: 8, 6: 9}.get(j, j + 2)))
                        for k in range(KC):
                            last = mm(PS[:, j % 6, 0:T], slot_in[:, j, k, s * P:(s + 1) * P], xT[:, k, :],
                                      start=(k == 0), stop=(k == KC - 1))
                        last.then_inc(proj_done, 1)
                    pe.wait_ge(xc_ok, g * SPG + (s + 1))
                    pe.wait_ge(wcur_ok, g * SPG + (s + 1))
                    pe.wait_ge(gates_taken, g * (2 * SPG) + (2 * s + 2))
                    for a in range(2):
                        mm(PS[:, 6 + a, 0:T], wcur[:, a, :], xc, start=True, stop=True).then_inc(gates_done, 1)

            pe.wait_ge(proj_taken, KC + 7 * KC)
            for t, (t0, n) in enumerate(TILES):
                for k in range(KC):
                    if t == 0:
                        pe.wait_ge(block_ok, k + 2)
                        pe.wait_ge(wout_in[k // 2], 16)
                    for a in range(2):
                        last = mm(PS[0:n, 2 * t + a, :], mixT[:, k, t0:t0 + n],
                                  slot_out[:, k // 2, k % 2, a * HALF:(a + 1) * HALF],
                                  start=(k == 0), stop=(k == KC - 1))
                last.then_inc(wout_done, 1)
            pe.wait_ge(gates_taken, 2 + 2 * KC)
            for k in range(KC):
                last = pe.transpose(PS[0:54, 6 + k // 4, (k % 4) * P:(k % 4 + 1) * P], so[:, k, :], ident[:, :])
            last.then_inc(so_turned, 1)
            for t, (t0, n) in enumerate(TILES):
                pe.wait_ge(x1_ok, t + 1)
                if t == 0:
                    pe.wait_ge(so_ok, 1)
                b = (6, 0, 2)[t]
                for k in range(KC):
                    last = pe.transpose(PS[:, b + k // 4, (k % 4) * P:(k % 4) * P + n],
                                        x1[0:n, t, k * P:(k + 1) * P], ident[0:n, 0:n])
                last.then_inc(x1_turned, 1)
            pe.wait_ge(misc_in, 32)
            for t, (t0, n) in enumerate(TILES):
                pe.wait_ge(x1T_ok, t + 1)
                for k in range(KC):
                    last = mm(PS[0:n, 4, t * NE:(t + 1) * NE], xT[:, k, t0:t0 + n], rw[:, k, :],
                              start=(k == 0), stop=(k == KC - 1))
            last.then_inc(lg_done, 1)
            pe.wait_ge(mask_ok, 1)
            for t in range(4):
                terms = [(ones, u) for u in range(min(t, 3))] + ([(upper, t)] if t < 3 else [])
                for q, (m, u) in enumerate(terms):
                    last = mm(PS[:, 5, t * NE:(t + 1) * NE], m[:, :], mask[:, u, :],
                              start=(q == 0), stop=(q == len(terms) - 1))
            last.then_inc(rank_done, 1)
            pe.wait_ge(gate_ok, 1)
            for t, (t0, n) in enumerate(TILES):
                last = pe.transpose(PS[0:NE, 6, t0:t0 + n], gate[0:n, t, :], ident[0:n, 0:n])
            last.then_inc(g_turned, 1)

            def gather(count):
                pe.wait_ge(oh_ok, count)
                for t, (t0, n) in enumerate(TILES):
                    for a in range(2):
                        last = mm(PS[64 * a:64 * a + 64, XB, :], onehot[0:n, t, :],
                                  x1[0:n, t, a * HALF:(a + 1) * HALF], start=(t == 0), stop=(t == 2))
                last.then_inc(xg_done, 1)

            def turn(src, done):
                for j in range(4):
                    last = pe.transpose(PS[:, TB, j * P:(j + 1) * P], src[:, j * P:(j + 1) * P], ident[:, :])
                last.then_inc(done, 1)

            def combine(t, par):
                t0, n = TILES[t]
                for a in range(2):
                    last = mm(PS[0:n, CB[t] + a, :], gt_sb[64 * a:64 * a + 64, par, t0:t0 + n],
                              y_sb[64 * a:64 * a + 64, :], start=True, stop=True)
                last.then_inc(c_done, 1)

            gather(1)
            pe.wait_ge(xg_ok, 1)
            turn(xg_sb, tx_done)
            pe.wait_ge(bias_in, 32)
            pe.wait_ge(gT_ok, 1)
            for t, (t0, n) in enumerate(TILES):
                if t == 2:
                    pe.wait_ge(c_taken, 1)
                for a in range(2):
                    last = mm(PS[0:n, CB[t] + a, :], gT[:, t0:t0 + n], bdn[:, a * HALF:(a + 1) * HALF],
                              start=True, stop=True)
                last.then_inc(c_done, 1)

            pe.wait_ge(items_ok, 1)
            n_pairs = pe.value_load(pairs[0:1, 0:1], min_val=NE // 2, max_val=(NE + MAX_EXTRA) // 2)
            with pe.Fori(0, n_pairs) as p:
                for s in range(2):
                    pe.wait_ge(xgT_ok, p * 2 + (s + 1))
                    for b in range(2):
                        for a in range(2):
                            mm(PS[64 * a:64 * a + 64, b, :], esel[:, s, :],
                               bgu[:, (2 * b + a) * HALF:(2 * b + a + 1) * HALF], start=True, stop=False)
                    for k in range(KC):
                        pe.wait_ge(gu_in[k], p * 32 + (16 * s + 16))
                        for b in range(2):
                            for a in range(2):
                                last = mm(PS[64 * a:64 * a + 64, b, :], xgT[:, k % 4, k // 4, :],
                                          ring_gu[:, k, (2 * b + a) * HALF:(2 * b + a + 1) * HALF],
                                          start=False, stop=(k == KC - 1))
                        last.then_inc(gu_used, 1)
                    pe.wait_ge(y_ok, p * 2 + (s + 1))
                    pe.wait_ge(c_taken, p * 6 + (3 * s + 3))
                    gather(p * 2 + (s + 2))
                    pe.wait_ge(cg_ok, p * 2 + (s + 1))
                    for t, (t0, n) in enumerate(TILES):
                        last = pe.transpose(PS[:, TB, t0:t0 + n], cgate[0:n, t, :, :], ident[0:n, 0:n])
                    last.then_inc(gt_done, 1)
                    combine(2, 1 - s)
                    pe.wait_ge(gt_ok, p * 2 + (s + 2))
                    pe.wait_ge(xg_ok, p * 2 + (s + 2))
                    turn(xg_sb, tx_done)
                    combine(1, 1 - s)
                    pe.wait_ge(xgT_ok, p * 2 + (s + 2))
                    pe.wait_ge(h_ok, p * 2 + (s + 1))
                    turn(up, ht_done)
                    pe.wait_ge(c_taken, p * 6 + (3 * s + 4))
                    combine(0, 1 - s)
                    pe.wait_ge(hT_ok, p * 2 + (s + 1))
                    for k in range(KC):
                        u = 4 * s + k // 2
                        if k % 2 == 0:
                            pe.wait_ge(dn_in[u], p * 16 + 16)
                        for a in range(2):
                            o = (k % 2) * D + a * HALF
                            last = mm(PS[64 * a:64 * a + 64, XB, :], hT[:, k % 4, k // 4, :],
                                      ring_dn[:, u, o:o + HALF], start=(k == 0), stop=(k == KC - 1))
                        if k % 2 == 1:
                            last.then_inc(dn_used, 1)
            pe.wait_ge(y_ok, n_pairs * 2 + 1)
            pe.wait_ge(c_taken, n_pairs * 6 + 3)
            combine(1, 1)
            combine(2, 1)
            pe.wait_ge(c_taken, n_pairs * 6 + 5)
            combine(0, 1)

        @block.vector
        def _(dve):
            link = Chain(dve, dve_own)
            dve.memset(xa_p[:, 0:3], 0.0).then_inc(xa_free, 1)
            link(dve.memset(cv_p[:, 0:2], 0.0))
            dve.wait_ge(gates_taken, 1)
            dve.tensor_scalar(bhalf[:, :], prm[:, BIN + MA * KC:BIN + (MA + 2) * KC], 0.5, None, ALU.mult)
            dve.tensor_scalar(ghalf[:, :], prm[:, LBA:LBA + 2 * KC], 0.5, None, ALU.mult)
            lam = prm[:, LAM:LAM + KC]
            ez, ab, s1, q = (spt[:, k, :] for k in range(4))
            link(dve.tensor_scalar(q, lam, -1.0, None, ALU.mult))
            dve.tensor_tensor(ab, lam, q, ALU.max).then_inc(prm_ok, 1)
            link(dve.tensor_scalar(sp2[:, :], q, 0.0, None, ALU.max))
            dve.wait_ge(prm_ok, 2)
            link(dve.tensor_scalar(s1, ez, 2.0, None, ALU.add))
            link(dve.reciprocal(q, s1))
            link(dve.tensor_tensor(s1, ez, q, ALU.mult))
            link(dve.tensor_tensor(ab, s1, s1, ALU.mult))
            link(dve.tensor_scalar(q, ab, 1.0 / 17, None, ALU.mult))
            for d in range(15, 1, -2):
                link(dve.scalar_tensor_tensor(out=q, in0=q, scalar=1.0 / d, in1=ab, op0=ALU.add, op1=ALU.mult))
            link(dve.scalar_tensor_tensor(out=q, in0=q, scalar=1.0, in1=s1, op0=ALU.add, op1=ALU.mult))
            link(dve.scalar_tensor_tensor(out=q, in0=q, scalar=2.0, in1=sp2[:, :], op0=ALU.mult, op1=ALU.add))
            dve.tensor_scalar(sp2[:, :], q, 2.0, None, ALU.mult).then_inc(prm_ok, 1)
            dve.wait_ge(gates_taken, 2)
            dve.memset(small[:, :], 0.0).then_inc(block_ok, 1)

            def par(col, c):
                return prm[:, ds(c + col, 1)]

            def stt(out, in0, scalar, in1, op0, op1):
                return dve.scalar_tensor_tensor(out=out, in0=in0, scalar=scalar, in1=in1, op0=op0, op1=op1)

            with dve.Fori(0, NG) as g:
                start, off = link.n, link.off
                link.off = g * K_DENSE + off
                for s in range(SPG):
                    c = g * SPG + s

                    def taken(j):
                        dve.wait_ge(proj_taken, g * (7 * SPG) + (KC + 7 * s + j))

                    def state(lo, n):
                        return stT[:, ds(c, 1), lo:lo + n].rearrange("p a r -> p (a r)")

                    def rows_of(lo, n):
                        return so[:, ds(c, 1), lo:lo + n].rearrange("p a r -> p (a r)")

                    def by_seq(ap, j):
                        return ap.rearrange("p (b j) -> p b j", j=j)

                    link(dve.tensor_copy(xa_s[:, :, 0:3], by_seq(state(8, 24), 3)))
                    taken(1)
                    dve.tensor_scalar(pr(xc), xa_p[:, 0:SEQ], par(CAW, c), par(CAB, c), ALU.mult, ALU.add)
                    link(dve.tensor_scalar(sm(xc), xa_s[:, :, 0:DS], par(CAW, c), par(CAB, c), ALU.mult, ALU.add))
                    for j in range(1, 4):
                        stt(pr(xc), xa_p[:, j:j + SEQ], par(CAW + 8 * j, c), pr(xc), ALU.mult, ALU.add)
                        last = stt(sm(xc), xa_s[:, :, j:j + DS], par(CAW + 8 * j, c), sm(xc), ALU.mult, ALU.add)
                        if j < 3:
                            link(last)
                    last.then_inc(xc_ok, 1)
                    dve.tensor_copy(rows_of(9, 3), xa_p[:, SEQ:SEQ + 3])
                    dve.tensor_copy(by_seq(rows_of(12, 24), 3), xa_s[:, :, DS:DS + 3]).then_inc(xa_free, 1)
                    dve.tensor_copy(cv_s[:, :, 0:2], by_seq(state(32, 16), 2))
                    taken(3)
                    dve.tensor_tensor(cv_p[:, 2:2 + SEQ], pr(cgt), pr(vt), ALU.mult)
                    link(dve.tensor_tensor(cv_s[:, :, 2:2 + DS], sm(cgt), sm(vt), ALU.mult))
                    dve.tensor_scalar(pr(uc), cv_p[:, 0:SEQ], par(CBW, c), None, ALU.mult)
                    link(dve.tensor_scalar(sm(uc), cv_s[:, :, 0:DS], par(CBW, c), None, ALU.mult))
                    for j in range(1, 3):
                        stt(pr(uc), cv_p[:, j:j + SEQ], par(CBW + 8 * j, c), pr(uc), ALU.mult, ALU.add)
                        link(stt(sm(uc), cv_s[:, :, j:j + DS], par(CBW + 8 * j, c), sm(uc), ALU.mult, ALU.add))
                    dve.tensor_copy(rows_of(36, 2), cv_p[:, SEQ:SEQ + 2])
                    link(dve.tensor_copy(by_seq(rows_of(38, 16), 2), cv_s[:, :, DS:DS + 2]))
                    taken(7)
                    link(stt(tmb, tmb, 1.0, bgt, ALU.add, ALU.mult))
                    link(dve.tensor_tensor(tmb, tmb, uc, ALU.mult))
                    link(stt(tma, tma, 1.0, gel, ALU.add, ALU.mult))
                    dve.wait_ge(t_ok, g * SPG + (s + 1))
                    dve.wait_ge(xc_ok, g * SPG + (s + 1))
                    stt(ti, ti, 1.0, xc, ALU.add, ALU.mult)
                    link(dve.tensor_scalar(aa, tr, 1.0, None, ALU.add))
                    link(dve.reciprocal(rr, aa))
                    dve.wait_ge(sq_ok, g * SPG + (s + 1))
                    dve.tensor_scalar(aa, rr, 2.0, -1.0, ALU.mult, ALU.add)
                    link(dve.tensor_tensor(sq, sq, rr, ALU.mult))
                    link(dve.tensor_tensor(ti, ti, sq, ALU.mult))
                    link(dve.tensor_tensor(small[:, :], sm(aa)[:, :, 0], state(0, 8), ALU.mult))
                    dve.memset(sm(aa)[:, :, 0], 0.0)
                    link(dve.tensor_tensor(sm(ti)[:, :, 0], sm(ti)[:, :, 0], small[:, :], ALU.add))
                    link(dve.tensor_tensor_scan(hh, aa, ti, 0.0, ALU.mult, ALU.add))
                    dve.tensor_copy(rows_of(0, 1), hh[:, SEQ - 1:SEQ])
                    dve.tensor_copy(rows_of(1, 8), sm(hh)[:, :, DS - 1])
                    link(dve.tensor_tensor(tma, tma, hh, ALU.mult))
                    dve.tensor_tensor(mixT[:, ds(c, 1), :].rearrange("p a t -> p (a t)"), tma, tmb, ALU.add)\
                       .then_inc(block_ok, 1)
                assert link.n - start == K_DENSE, link.n - start
                link.n = start
                link.off = off
            link.off = NG * K_DENSE

            def normalise(t, n, src, count):
                dve.bn_stats(stat[0:n, t, 0, :], src[0:n, t, 0:HALF])
                link(dve.bn_stats(stat[0:n, t, 1, :], src[0:n, t, HALF:D]))
                link(dve.bn_aggr(mv[0:n, t, 0:2], stat[0:n, t, :, :]))
                dve.tensor_scalar(mv[0:n, t, 2:3], mv[0:n, t, 1:2], (4 if count < 3 else 1) * EPS, None, ALU.add)\
                   .then_inc(var_ok, 1)
                dve.wait_ge(var_ok, count + 1)
                dve.wait_ge(std_ok, count + 1)
                v, r, w = (mv[0:n, t, k:k + 1] for k in (2, 4, 5))
                link(dve.reciprocal(r, mv[0:n, t, 3:4]))
                link(dve.tensor_tensor(w, r, r, ALU.mult))
                link(dve.tensor_tensor(w, w, v, ALU.mult))
                link(dve.tensor_scalar(w, w, -0.5, 1.5, ALU.mult, ALU.add))
                link(dve.tensor_tensor(r, r, w, ALU.mult))
                link(dve.tensor_scalar(x1[0:n, t, :], src[0:n, t, :], mv[0:n, t, 0:1], r, ALU.subtract, ALU.mult))
                link(dve.tensor_tensor(x1[0:n, t, :], x1[0:n, t, :], ln_g[0:n, :], ALU.mult))
                return dve.tensor_tensor(x1[0:n, t, :], x1[0:n, t, :], ln_b[0:n, :], ALU.add)

            dve.wait_ge(wcur_ok, KC)
            dve.wait_ge(ln_in, 32)
            for t, (t0, n) in enumerate(TILES):
                dve.wait_ge(wout_done, t + 1)
                link(stt(x1[0:n, t, :].rearrange("p (a n) -> p a n", a=2),
                         x_tok[0:n, t, :].rearrange("p (a n) -> p a n", a=2), 2 * ALPHA,
                         PS[0:n, 2 * t:2 * t + 2, :], ALU.mult, ALU.add))
                normalise(t, n, x1, t).then_inc(x1_ok, 1)

            dve.wait_ge(so_out, 96)
            dve.memset(lg[:, 2, :], 0.0)
            dve.memset(tabf[0:1, :, :], 0.0)
            dve.wait_ge(lg_done, 1)
            dve.wait_ge(misc_in, 32)
            dve.wait_ge(x1_ok, 3)
            dve.tensor_tensor(lg[:, 0:2, :], PS[:, 4, 0:2 * NE].rearrange("p (t e) -> p t e", t=2),
                              rb[:, :].unsqueeze(1).to_broadcast([P, 2, NE]), ALU.add)
            link(dve.tensor_copy(small[:, 0:1], ones[:, 0:1]))
            link(dve.tensor_tensor(lg[0:NS, 2, :], PS[0:NS, 4, 2 * NE:3 * NE], rb[0:NS, :], ALU.add))
            for t in range(3):
                last = dve.max(top[:, t, :], lg[:, t, :])
            link(last)
            for t in range(3):
                last = dve.max_index(idx[:, t, :], top[:, t, :], lg[:, t, :])
            link(last)
            dve.tensor_copy(idf, idx)
            dve.tensor_tensor(ek, top[:, :, 0:TOPK], top[:, :, 0:1].to_broadcast([P, 3, TOPK]), ALU.subtract)\
               .then_inc(top_ok, 1)
            dve.wait_ge(top_ok, 1)
            for t in range(3):
                last = dve.tensor_tensor(oh4[:, t], iota[:, 0:NE].unsqueeze(1).to_broadcast([P, TOPK, NE]),
                                         idf[:, t, 0:TOPK].unsqueeze(2).to_broadcast([P, TOPK, NE]), ALU.is_equal)
            link(last)
            for t in range(3):
                last = dve.tensor_reduce(mask[:, t, :], oh4[:, t].rearrange("p k e -> p e k"), AX_X, ALU.add)
            link(last)
            dve.memset(mask[NS:P, 2, :], 0.0).then_inc(mask_ok, 1)
            dve.wait_ge(exp_ok, 1)
            link(dve.tensor_reduce(es, ek, AX_X, ALU.add))
            link(dve.reciprocal(es, es))
            link(dve.tensor_tensor(ek, ek, es.unsqueeze(2).to_broadcast([P, 3, TOPK]), ALU.mult))
            for t in range(3):
                last = dve.tensor_tensor(og4[:, t], oh4[:, t],
                                         ek[:, t, :].unsqueeze(2).to_broadcast([P, TOPK, NE]), ALU.mult)
            link(last)
            for t in range(3):
                last = dve.tensor_reduce(gate[:, t, :], og4[:, t].rearrange("p k e -> p e k"), AX_X, ALU.add)
            link(last)
            dve.memset(gate[NS:P, 2, :], 0.0).then_inc(gate_ok, 1)
            dve.wait_ge(gate_ok, 1)
            dve.tensor_scalar(gateh[:, :, :], gate[:, :, :], 0.5, None, ALU.mult)
            dve.wait_ge(rank_done, 1)
            dve.tensor_copy(cnt, PS[:, 5, 3 * NE:4 * NE])
            link(stt(posm[:, :, :], PS[:, 5, 0:3 * NE].rearrange("p (t e) -> p t e", t=3), 1.0, mask, ALU.add, ALU.mult))
            link(dve.tensor_scalar(posm[:, :, :], posm[:, :, :], -1.0, None, ALU.add))

            def pick(e, b, par):
                for t in range(3):
                    dve.tensor_scalar(onehot[:, t, :], iota[:, ds(b * ROWS, ROWS)], posm[:, t, ds(e, 1)], None, ALU.is_equal)
                dve.tensor_copy(esel[:, par, :], ident[0:NE, ds(e, 1)].to_broadcast([NE, ROWS])).then_inc(oh_ok, 1)

            def weigh(e, b):
                for t in range(3):
                    last = dve.tensor_scalar(cgate[:, t, :, :],
                                             iota[:, ds(b * ROWS, ROWS)].unsqueeze(1).to_broadcast([P, 2, ROWS]),
                                             posm[:, t, ds(e, 1)], gateh[:, t, ds(e, 1)], ALU.is_equal, ALU.mult)
                last.then_inc(cg_ok, 1)

            pick(0, 0, 0)
            weigh(0, 0)
            link(dve.tensor_scalar(ext, cnt, float(ROWS), None, ALU.is_gt))
            for b in range(2, NB):
                link(stt(ext, cnt, float(b * ROWS), ext, ALU.is_gt, ALU.add))
            link(dve.tensor_tensor_scan(incl, ones[:, 0:NE], ext, 0.0, ALU.mult, ALU.add))
            link(dve.tensor_tensor(excl, incl, ext, ALU.subtract))
            nq = 22

            def by_q(ap):
                return ap.unsqueeze(1).to_broadcast([1, nq, NE])
            qs = iota[0:1, 0:nq].unsqueeze(2).to_broadcast([1, nq, NE])
            dve.tensor_tensor(tb0, by_q(excl[0:1, :]), qs, ALU.is_le)
            link(dve.tensor_tensor(tb1, by_q(incl[0:1, :]), qs, ALU.is_gt))
            link(dve.tensor_tensor(tb0, tb0, tb1, ALU.mult))
            link(dve.tensor_tensor(tb1, tb0, by_q(iota[0:1, 0:NE]), ALU.mult))
            link(dve.tensor_reduce(tabf[0:1, 0, NE:NE + nq], tb1, AX_X, ALU.add))
            link(dve.tensor_tensor(tb1, qs, by_q(excl[0:1, :]), ALU.subtract))
            link(stt(tb1, tb1, float(1 - NB), tb0, ALU.add, ALU.mult))
            link(dve.tensor_reduce(tabf[0:1, 1, NE:NE + nq], tb1, AX_X, ALU.add))
            dve.tensor_copy(tabf[0:1, 0, 0:NE], iota[0:1, 0:NE])
            dve.tensor_scalar(prf[0:1, 0:10], iota[0:1, 0:20:2], incl[0:1, NE - 1:NE], None, ALU.is_lt)
            link(dve.tensor_scalar(tabf[0:1, 1, NE:NE + nq], tabf[0:1, 1, NE:NE + nq], float(NB), None, ALU.add))
            link(dve.tensor_reduce(prf[0:1, 10:11], prf[0:1, 0:10], AX_X, ALU.add))
            link(dve.tensor_scalar(prf[0:1, 11:12], prf[0:1, 10:11], float(NE // 2), None, ALU.add))
            dve.tensor_copy(pairs[0:1, 0:1], prf[0:1, 11:12])
            link(dve.tensor_copy(items[0:1, :, :], tabf[0:1, :, 0:64]))
            dve.memset(gt_sb[:, 1, :], 0.0).then_inc(gt_ok, 1)
            dve.memset(y_sb, 0.0).then_inc(y_ok, 1)
            dve.tensor_copy(small[:, 0:1], ones[:, 0:1]).then_inc(items_ok, 1)

            def halves(ap):
                return ap.rearrange("p (a n) -> p a n", a=2)

            def add(t, scale, src, count):
                n = TILES[t][1]
                dve.wait_ge(c_done, count)
                return stt(halves(y_acc[0:n, t, :]), halves(src[0:n, t, :]), scale,
                           PS[0:n, CB[t]:CB[t] + 2, :], ALU.mult, ALU.add).then_inc(c_taken, 1)

            for t in range(3):
                add(t, ALPHA, x1, t + 1)

            n_pairs = dve.value_load(pairs[0:1, 0:1], min_val=NE // 2, max_val=(NE + MAX_EXTRA) // 2)
            with dve.Fori(0, n_pairs) as p:
                start, off = link.n, link.off
                link.off = p * K_PAIR + off
                for s in range(2):
                    e = dve.value_load(items[0:1, 0, ds(p * 2 + (s + 1), 1)], min_val=0, max_val=NE - 1)
                    b = dve.value_load(items[0:1, 1, ds(p * 2 + (s + 1), 1)], min_val=0, max_val=NB)
                    dve.wait_ge(xg_done, p * 2 + (s + 1))
                    pick(e, b, 1 - s)
                    dve.wait_ge(gu_used, p * 16 + (8 * s + 8))
                    dve.tensor_scalar(gm, PS[:, 0, :], LIMIT, None, ALU.min).then_inc(gm_ok, 1)
                    link(dve.tensor_scalar(up, PS[:, 1, :], LIMIT, -LIMIT, ALU.min, ALU.max))
                    dve.wait_ge(th_ok, p * 2 + (s + 1))
                    link(stt(th, th, 1.0, gm, ALU.add, ALU.mult))
                    stt(up, up, 1.0, th, ALU.add, ALU.mult).then_inc(h_ok, 1)
                    dve.wait_ge(c_taken, p * 6 + (3 * s + 3))
                    for q, t in enumerate((2, 1, 0)):
                        add(t, 1.0, y_acc, p * 6 + (3 * s + q + 4))
                    dve.wait_ge(gt_done, p * 2 + (s + 1))
                    weigh(e, b)
                assert link.n - start == K_PAIR, link.n - start
                link.n = start
                link.off = off
            dve.wait_ge(c_taken, n_pairs * 6 + 3)
            dve.wait_ge(ln2_in, 32)
            link = Chain(dve, dve_end)
            for q, t in enumerate((1, 2, 0)):
                add(t, 1.0, y_acc, n_pairs * 6 + (q + 4))
                dve.wait_ge(c_taken, n_pairs * 6 + (q + 4))
                link(dve.tensor_copy(small[:, 1:2], ones[:, 0:1]))
                normalise(t, TILES[t][1], y_acc, q + 3).then_inc(out_ok, 1)


_INS = ["x_prompt", "x_sample", "state_rglru_h", "state_rglru_conv", "state_shortconv", "w_in", "b_in", "conv_a_w",
        "conv_a_b", "lru_wa", "lru_ba", "lru_wx", "lru_bx", "lru_lambda", "conv_b_w", "w_out", "ln1_g", "ln1_b",
        "router_w", "router_b", "w_gu", "b_gu", "w_down", "b_down", "ln2_g", "ln2_b"]
_OUTS = [(1, SEQ, D), (DB, DS, D), (1, 1, D), (1, 1, 3, D), (1, 1, 2, D), (1, DB, D), (1, DB, 3, D), (1, DB, 2, D)]


def kernel(**inputs):
    import numpy as _np
    import concourse.bacc as _bacc
    from concourse import mybir as _mybir
    from concourse.bass_utils import run_bass_kernel_spmd as _run

    nc = _bacc.Bacc("TRN2", target_bir_lowering=False, num_devices=1)
    arrays, args = {}, []
    for name in _INS:
        a = _np.ascontiguousarray(inputs[name])
        arrays[f"in_{name}"] = a
        args.append(nc.dram_tensor(f"in_{name}", a.shape, _mybir.dt.from_np(a.dtype), kind="ExternalInput").ap())
    for i, shape in enumerate(_OUTS):
        args.append(nc.dram_tensor(f"out_{i}", shape, _mybir.dt.float32, kind="ExternalOutput").ap())
    hybrid_layer(nc, *args)
    r = _run(nc, [arrays], core_ids=[0])
    return tuple(r.results[0][f"out_{i}"] for i in range(len(_OUTS)))
```

```python
from contextlib import ExitStack

import concourse.bass as bass
from concourse import mybir

P = 128
D = 1024
KC = D // P
SEQ, DB, DS = 256, 8, 8
NS = DB * DS
T = SEQ + NS
TILES = [(0, P), (P, P), (2 * P, NS)]
IN_W = 7 * D
NP = 7 * KC
RING = 4
PB = 4
AHEAD = 3
NE, TOPK, FF = 32, 4, 1024
ROWS = 64
MAX_EXTRA = T * TOPK // ROWS
NB = (T + ROWS - 1) // ROWS
HALF = 512
ALPHA = 2.0 ** 0.25
EPS = 1e-5
LIMIT, SW_ALPHA = 7.0, 1.702

XA, GA, BG, CG, V, MA, MB = range(7)
ORDER = [XA, CG, V, GA, BG, MA, MB]
CAW, CAB, LBA, LBX, LAM, CBW, BIN = 0, 32, 40, 48, 56, 64, 88
NPRM = BIN + 7 * KC

ALU = mybir.AluOpType
ACT = mybir.ActivationFunctionType
AX_X = mybir.AxisListType.X
F32 = mybir.dt.float32
F32R = mybir.dt.float32r
I32 = mybir.dt.int32
U32 = mybir.dt.uint32
ds = bass.ds


XB, TB, CB = 2, 3, (4, 6, 4)
LAST_SUMS = ((1, 6), (2, 4), (0, 0))
K_DENSE, K_PAIR = 20, 4


class Chain:

    def __init__(self, eng, sem):
        self.eng, self.sem, self.n, self.off = eng, sem, 0, 0

    def __call__(self, ins):
        ins.then_inc(self.sem, 1)
        self.n += 1
        self.eng.wait_ge(self.sem, self.off + self.n)


def hybrid_layer(nc, x_prompt, x_sample, state_h, state_conv, state_sc, w_in, b_in, conv_a_w,
                 conv_a_b, lru_wa, lru_ba, lru_wx, lru_bx, lru_lambda, conv_b_w, w_out, ln1_g,
                 ln1_b, router_w, router_b, w_gu, b_gu, w_down, b_down, ln2_g, ln2_b,
                 y_prompt, y_sample, h_prompt, conv_prompt, sc_prompt, h_sample, conv_sample,
                 sc_sample):
    ctx = ExitStack()
    with ctx:
        def sb(name, shape, dt=F32):
            return ctx.enter_context(nc.sbuf_tensor(name, shape, dt))

        def sem(name):
            return ctx.enter_context(nc.semaphore(name))

        base = -(-nc.sbuf_base // 32) * 32
        size = (nc.sbuf_usable_end - base) // 32 * 32
        ctx.enter_context(nc.sbuf_tensor("arena", [P, size // 4], F32))
        slot = 8 * D
        GU, DN = 0, 10 * slot
        XT, X1 = DN + 8 * slot, DN + 8 * slot + 12 * D
        MID = X1 + 12 * D
        at = [MID + 30 * D]

        def place(name, shape, offset, dt=F32):
            return nc.alloc_sbuf_tensor_at(name, shape, dt, offset=base + offset)

        def small_tile(name, shape, dt=F32):
            n = 4
            for d in shape[1:]:
                n *= d
            at[0] += -(-n // 32) * 32
            assert at[0] <= size, at[0] - size
            return place(name, shape, at[0] - -(-n // 32) * 32, dt)

        ring_gu = place("ring_gu", [P, 10, 2 * FF], GU)
        ring_dn = place("ring_dn", [P, 8, 2 * D], DN)

        def gu_slot(s, k):
            return 8 + k if s == 1 and k < 2 else k

        raw = place("raw", [P, RING, KC, P], DN)
        w_hi = place("w_hi", [P, RING, KC, P], DN + 2 * slot, F32R)
        w_lo = place("w_lo", [P, RING, KC, P], DN + 4 * slot, F32R)
        dsm = place("dsm", [P, 2 * D], DN + 7 * slot)
        dat = [0]

        def in_dsm(n):
            dat[0] += n
            assert dat[0] <= 2 * D
            return dsm[:, dat[0] - n:dat[0]]
        xa_pad, cv_pad = in_dsm(347), in_dsm(338)
        vrows = in_dsm(2 * P).rearrange("p (a n) -> p a n", a=2)
        prm = in_dsm(NPRM)
        bhalf = in_dsm(2 * KC)
        ghalf = in_dsm(2 * KC)
        sp2 = in_dsm(KC)
        spt = in_dsm(4 * KC).rearrange("p (a c) -> p a c", a=4)
        stT = in_dsm(KC * 48).rearrange("p (c r) -> p c r", c=KC)
        so = in_dsm(KC * 54).rearrange("p (c r) -> p c r", c=KC)

        x_tok = place("x_tok", [P, 3, D], XT)
        x1 = place("x1", [P, 3, D], X1)
        y_acc = x_tok
        wab = x1[:, 0:2, :].rearrange("p a (c n) -> p a c n", c=KC)
        st_rows = x1[:, 2, :]

        x_hi = place("x_hi", [P, KC, T], MID, F32R)
        x_lo = place("x_lo", [P, KC, T], MID + 10 * D, F32R)
        mixT = place("mixT", [P, KC, T], MID + 20 * D)
        xT = place("xT", [P, KC, T], MID)
        so_rows = place("so_rows", [54, D], MID + 10 * D)
        brow = place("brow", [2 * NE, 2 * FF], MID + 20 * D)
        bgu, bdn = brow[0:NE, :], brow[NE:2 * NE, 0:D]
        gT = place("gT", [2 * NE, T], MID + 28 * D)[NE:2 * NE, :]

        ident = small_tile("ident", [P, P])
        upper = small_tile("upper", [P, P])
        ones = small_tile("ones", [P, P])
        iota = small_tile("iota", [P, (NB + 1) * ROWS])
        rw = small_tile("rw", [P, KC, NE])
        rb = small_tile("rb", [P, NE])
        posm = small_tile("posm", [P, 3, NE])
        gate = small_tile("gate", [P, 3, NE])
        gateh = small_tile("gateh", [P, 3, NE])
        gt_sb = small_tile("gt_sb", [P, 2, T])
        items = small_tile("items", [1, 2, 64], I32)
        pairs = small_tile("pairs", [1, 4], I32)
        stat = small_tile("stat", [P, 3, 2, 6])
        mv = small_tile("mv", [P, 3, 8])
        small = small_tile("small", [P, 8])

        PS = ctx.enter_context(nc.psum_tensor("PS", [P, 8, HALF], F32))

        tiles = place("tiles", [P, 12 * T + 2 * P], GU + 8 * slot)
        bgt, cgt, vt, gel, tma, tmb, xc, tr, ti, rr, aa, sq = (tiles[:, i * T:(i + 1) * T] for i in range(12))
        wcur = tiles[:, 12 * T:12 * T + 2 * P].rearrange("p (a n) -> p a n", a=2)
        hh = vt
        uc = cgt
        xa_p, xa_s = xa_pad[:, 0:259], xa_pad[:, 259:347].rearrange("p (b s) -> p b s", b=DB)
        cv_p, cv_s = cv_pad[:, 0:258], cv_pad[:, 258:338].rearrange("p (b s) -> p b s", b=DB)

        def pr(t):
            return t[:, 0:SEQ]

        def sm(t):
            return t[:, SEQ:T].rearrange("p (b s) -> p b s", b=DB)

        mid = place("mid", [P, 20 * D // 4], MID)
        xg_sb, xgT_f, y_sb, hT_f = (mid[:, i * HALF:(i + 1) * HALF] for i in range(4))
        xgT = xgT_f.rearrange("p (j a r) -> p j a r", j=4, a=2)
        hT = hT_f.rearrange("p (j a r) -> p j a r", j=4, a=2)
        onehot = mid[:, 2048:2240].rearrange("p (t r) -> p t r", t=3)
        cgate = mid[:, 2240:2624].rearrange("p (t a r) -> p t a r", t=3, a=2)
        esel = mid[0:NE, 2624:2752].rearrange("p (s r) -> p s r", s=2)
        gm, th, up = (mid[:, 2752 + i * HALF:2752 + (i + 1) * HALF] for i in range(3))
        rat = [4288]

        def route(n):
            rat[0] += n
            assert rat[0] <= 5 * D
            return mid[:, rat[0] - n:rat[0]]
        lg = route(96).rearrange("p (t e) -> p t e", t=3)
        mask = route(96).rearrange("p (t e) -> p t e", t=3)
        cnt, ext, incl, excl = (route(32) for _ in range(4))
        top = route(24).rearrange("p (t k) -> p t k", t=3)
        idx = route(24).bitcast(U32).rearrange("p (t k) -> p t k", t=3)
        idf = route(24).rearrange("p (t k) -> p t k", t=3)
        ek = route(12).rearrange("p (t k) -> p t k", t=3)
        es = route(3)
        tabf = route(128).rearrange("p (a q) -> p a q", a=2)
        prf = route(12)
        oh4 = mid[:, 2752:3136].rearrange("p (t k e) -> p t k e", t=3, k=TOPK)
        og4 = mid[:, 3136:3520].rearrange("p (t k e) -> p t k e", t=3, k=TOPK)
        tb0 = mid[0:1, 2752:2752 + 22 * NE].rearrange("p (q e) -> p q e", q=22)
        tb1 = mid[0:1, 3520:3520 + 22 * NE].rearrange("p (q e) -> p q e", q=22)

        x_in = sem("x_in")
        prm_in, st_in, wab_in, misc_in, ln_in = (sem(n) for n in
                                                 ("prm_in", "st_in", "wab_in", "misc_in", "ln_in"))
        raw_in = [sem(f"raw_in{j}") for j in range(RING)]
        hi_ok, lo_ok = sem("hi_ok"), sem("lo_ok")
        wout_in = [sem(f"wout_in{j}") for j in range(4)]
        bias_in = sem("bias_in")
        ln2_in = sem("ln2_in")
        gu_in = [sem(f"gu_in{k}") for k in range(10)]
        dn_in = [sem(f"dn_in{k}") for k in range(8)]
        const_ok, zero_ok, pool_own = sem("const_ok"), sem("zero_ok"), sem("pool_own")
        x_turned, prm_turned, st_turned = sem("x_turned"), sem("prm_turned"), sem("st_turned")
        proj_done, proj_taken = sem("proj_done"), sem("proj_taken")
        gates_done, gates_taken = sem("gates_done"), sem("gates_taken")
        wcur_ok = sem("wcur_ok")
        prm_ok = sem("prm_ok")
        xa_free, cv_free, xc_ok, block_ok = sem("xa_free"), sem("cv_free"), sem("xc_ok"), sem("block_ok")
        t_ok, sq_ok = sem("t_ok"), sem("sq_ok")
        xlo_ok = sem("xlo_ok")
        wout_done, r_taken = sem("wout_done"), sem("r_taken")
        so_turned, so_ok = sem("so_turned"), sem("so_ok")
        var_ok, std_ok, x1_ok = sem("var_ok"), sem("std_ok"), sem("x1_ok")
        x1_turned, x1T_ok, lg_done, lg_taken = (sem(n) for n in ("x1_turned", "x1T_ok", "lg_done", "lg_taken"))
        top_ok, exp_ok = sem("top_ok"), sem("exp_ok")
        mask_ok, rank_done, gate_ok = sem("mask_ok"), sem("rank_done"), sem("gate_ok")
        g_turned, gT_ok = sem("g_turned"), sem("gT_ok")
        items_ok = sem("items_ok")
        oh_ok, cg_ok = sem("oh_ok"), sem("cg_ok")
        xg_done, xg_ok, tx_done, xgT_ok = (sem(n) for n in ("xg_done", "xg_ok", "tx_done", "xgT_ok"))
        gt_done, gt_ok = sem("gt_done"), sem("gt_ok")
        gu_used, dn_used = sem("gu_used"), sem("dn_used")
        gm_ok, th_ok, h_ok, ht_done, hT_ok, y_ok = (
            sem(n) for n in ("gm_ok", "th_ok", "h_ok", "ht_done", "hT_ok", "y_ok"))
        c_done, c_taken = sem("c_done"), sem("c_taken")
        out_ok, out_sem, so_out = sem("out_ok"), sem("out_sem"), sem("so_out")
        dve_own, dve_end = sem("dve_own"), sem("dve_end")

        block = ctx.enter_context(nc.Block())

        win_v = w_in[0].rearrange("(k p) n -> p k n", p=P)
        wout_v = w_out[0].rearrange("(k p) n -> p k n", p=P)
        slot_out = ring_dn[:, 0:4, :].rearrange("p j (k n) -> p j k n", k=2)
        ln_g, ln_b = ring_dn[:, 6, 0:D], ring_dn[:, 6, D:2 * D]
        ln2g, ln2b = ring_gu[:, 0, 0:D], ring_gu[:, 0, D:2 * D]

        @block.sync
        def _(sp):
            sp.dma_start(x_tok[:, 0:2, :], x_prompt[0].rearrange("(t p) d -> p t d", p=P)).then_inc(x_in, 16)
            sp.dma_start(x_tok[0:NS, 2, :], x_sample.rearrange("b s d -> (b s) d")).then_inc(x_in, 16)

            def load_piece(q):
                if q >= RING:
                    sp.wait_ge(lo_ok, q - RING + 1)
                col = ORDER[q % 7] * D + (q // 7) * P
                sp.dma_start(raw[:, q % RING], win_v[:, :, col:col + P]).then_inc(raw_in[q % RING], 16)

            for q in range(2):
                load_piece(q)
            rows = 0
            for src, n in ((conv_a_w, 32), (conv_a_b, 8), (lru_ba, 8), (lru_bx, 8), (lru_lambda, 8), (conv_b_w, 24)):
                v = src[0] if n > 8 else src
                sp.dma_start(vrows[rows:rows + n, 0, :], v.rearrange("a (c p) -> (a c) p", p=P)).then_inc(prm_in, 16)
                rows += n
            sp.dma_start(vrows[0:7 * KC, 1, :], b_in.rearrange("a (c p) -> (a c) p", p=P)).then_inc(prm_in, 16)
            sp.dma_start(st_rows[0:8, :], state_h[0]).then_inc(st_in, 16)
            sp.dma_start(st_rows[8:32, :], state_conv[0].rearrange("b j d -> (b j) d")).then_inc(st_in, 16)
            sp.dma_start(st_rows[32:48, :], state_sc[0].rearrange("b j d -> (b j) d")).then_inc(st_in, 16)
            for q in range(2, 4):
                load_piece(q)
            sp.wait_ge(zero_ok, 1)
            for a, w in enumerate((lru_wa, lru_wx)):
                for j in range(2):
                    sp.dma_start(wab[64 * j:64 * j + 64, a, :, 64 * j:64 * j + 64],
                                 w[0].rearrange("(c j) i o -> j i c o", j=2)[j]).then_inc(wab_in, 16)
            for q in range(4, NP):
                load_piece(q)
                if q % 4 == 3 and q < 7 + 4 * KC:
                    k = (q - 7) // 4
                    sp.dma_start(ring_gu[:, k], w_gu[0, 0, k * P:(k + 1) * P, :]).then_inc(gu_in[k], 16)
            sp.dma_start(rw[:, :, :], router_w[0].rearrange("(k p) e -> p k e", p=P)).then_inc(misc_in, 16)
            sp.dma_start(rb[:, :], router_b[0:1, :].to_broadcast([P, NE])).then_inc(misc_in, 16)
            sp.dma_start(ln_g, ln1_g[0:1, :].to_broadcast([P, D])).then_inc(ln_in, 16)
            sp.dma_start(ln_b, ln1_b[0:1, :].to_broadcast([P, D])).then_inc(ln_in, 16)
            for j in range(4):
                if j < 2:
                    sp.wait_ge(lo_ok, NP - 2 + 2 * j)
                else:
                    sp.wait_ge(proj_done, NP - 6 + 2 * j)
                sp.dma_start(slot_out[:, j], wout_v[:, 2 * j:2 * j + 2, :]).then_inc(wout_in[j], 16)

            def load_gu(e, s, k):
                sp.dma_start(ring_gu[:, gu_slot(s, k)], w_gu[0, ds(e, 1), k * P:(k + 1) * P, :]
                             .rearrange("a p n -> p (a n)")).then_inc(gu_in[gu_slot(s, k)], 16)

            def load_dn(e, s, u):
                sp.dma_start(ring_dn[:, 4 * s + u, :].rearrange("p (k n) -> p k n", k=2),
                             w_down[0, ds(e, 1), 2 * u * P:(2 * u + 2) * P, :]
                             .rearrange("a (k p) n -> p (a k) n", p=P)).then_inc(dn_in[4 * s + u], 16)

            load_dn(1, 1, 0)
            load_dn(1, 1, 1)
            sp.wait_ge(block_ok, KC + 1)
            load_gu(1, 1, 0)
            load_gu(1, 1, 1)
            sp.wait_ge(wout_done, 3)
            for u in range(4):
                load_dn(0, 0, u)
            sp.dma_start(bgu, b_gu[0]).then_inc(bias_in, 16)
            sp.dma_start(bdn, b_down[0]).then_inc(bias_in, 16)
            sp.wait_ge(x1_ok, 3)
            load_dn(1, 1, 2)
            sp.wait_ge(so_turned, 1)
            load_dn(1, 1, 3)
            for k in range(2, KC):
                sp.wait_ge(gu_used, k + 1)
                load_gu(1, 1, k)

            def load_pair(before, experts):
                for s in range(2):
                    for k in range(8):
                        sp.wait_ge(gu_used, before * 16 + (8 * s + k + (9 if k >= 2 else 1)))
                        load_gu(experts[s], s, k)
                    for u in range(4):
                        sp.wait_ge(dn_used, before * 8 + (4 * s + u + 1))
                        load_dn(experts[s], s, u)

            with sp.Fori(0, NE // 2 - 1) as before:
                load_pair(before, [2 * before + 2, 2 * before + 3])
            sp.wait_ge(items_ok, 1)
            n_pairs = sp.value_load(pairs[0:1, 0:1], min_val=NE // 2, max_val=(NE + MAX_EXTRA) // 2)
            with sp.If(n_pairs > NE // 2):
                with sp.Fori(NE // 2 - 1, n_pairs - 1) as before:
                    ea = sp.value_load(items[0:1, 0, ds(2 * before + 2, 1)], min_val=0, max_val=NE - 1)
                    eb = sp.value_load(items[0:1, 0, ds(2 * before + 3, 1)], min_val=0, max_val=NE - 1)
                    load_pair(before, [ea, eb])
            sp.wait_ge(gu_used, n_pairs * 16)
            sp.dma_start(ln2g, ln2_g[0:1, :].to_broadcast([P, D])).then_inc(ln2_in, 16)
            sp.dma_start(ln2b, ln2_b[0:1, :].to_broadcast([P, D])).then_inc(ln2_in, 16)
            for q, t in enumerate((1, 2, 0)):
                t0, n = TILES[t]
                sp.wait_ge(out_ok, q + 1)
                dst = y_prompt[0, t0:t0 + n, :] if t < 2 else y_sample.rearrange("b s d -> (b s) d")
                sp.dma_start(dst, x1[0:n, t, :]).then_inc(out_sem, 16)
            sp.wait_ge(out_sem, 48)

        @block.gpsimd
        def _(pool):
            pool.memset(ident[:, :], 0.0).then_inc(pool_own, 1)
            pool.memset(upper[:, :], 1.0).then_inc(pool_own, 1)
            pool.memset(ones[:, :], 1.0).then_inc(const_ok, 1)
            pool.wait_ge(pool_own, 2)
            pool.affine_select(out=ident[:, :], in_=ident[:, :], compare_op=ALU.not_equal, fill=1.0,
                               base=0, pattern=[[-1, P]], channel_multiplier=1).then_inc(const_ok, 1)
            pool.affine_select(out=upper[:, :], in_=upper[:, :], compare_op=ALU.is_gt, fill=0.0,
                               base=0, pattern=[[1, P]], channel_multiplier=-1).then_inc(const_ok, 1)
            pool.memset(wab, 0.0).then_inc(zero_ok, 1)
            pool.iota(iota[:, :], pattern=[[1, (NB + 1) * ROWS]], base=0, channel_multiplier=0,
                      allow_small_or_imprecise_dtypes=True).then_inc(const_ok, 1)
            with pool.Fori(0, KC // PB) as g:
                for q in range(7 * PB):
                    pool.wait_ge(hi_ok, g * (7 * PB) + (q + 1))
                    pool.tensor_tensor(w_lo[:, q % RING], raw[:, q % RING], w_hi[:, q % RING].bitcast(F32),
                                       ALU.subtract).then_inc(lo_ok, 1)

        @block.scalar
        def _(act):
            def split_high(q):
                act.wait_ge(raw_in[q % RING], 16 * (q // RING + 1))
                if q >= RING:
                    act.wait_ge(proj_done, q - RING + 1)
                act.activation(w_hi[:, q % RING], raw[:, q % RING], ACT.Copy).then_inc(hi_ok, 1)

            for k in range(KC):
                act.wait_ge(x_turned, k + 1)
                act.activation(x_hi[:, k, :], PS[:, k % 6, 0:T], ACT.Copy).then_inc(proj_taken, 1)
                if k in (3, 5, 7):
                    split_high((k - 3) // 2)
            act.wait_ge(prm_turned, 1)
            act.activation(prm, PS[:, 6, 0:NPRM], ACT.Copy).then_inc(gates_taken, 1)
            act.wait_ge(st_turned, 1)
            act.activation(stT, PS[:, 7, 0:KC * 48].rearrange("p (k r) -> p k r", k=KC), ACT.Copy)\
               .then_inc(gates_taken, 1)
            act.wait_ge(prm_ok, 1)
            act.activation(spt[:, 0, :], spt[:, 1, :], ACT.Exp, scale=-1.0).then_inc(prm_ok, 1)
            act.wait_ge(prm_ok, 3)

            for q in range(NP):
                c, j = q // 7, q % 7
                m = ORDER[j]
                bias = prm[:, BIN + m * KC + c:BIN + m * KC + c + 1]
                if q + AHEAD < NP:
                    split_high(q + AHEAD)
                act.wait_ge(proj_done, q + 1)
                ps = PS[:, j % 6, 0:T]
                if m == XA:
                    act.wait_ge(xa_free, c + 1)
                    act.activation(xa_p[:, 3:259], pr(ps), ACT.Identity, bias=bias)
                    act.activation(xa_s[:, :, 3:11], sm(ps), ACT.Identity, bias=bias).then_inc(proj_taken, 1)
                elif m in (CG, V, BG):
                    if m == CG:
                        act.wait_ge(block_ok, c + 1)
                    act.activation({CG: cgt, V: vt, BG: bgt}[m], ps, ACT.Identity, bias=bias).then_inc(proj_taken, 1)
                elif m == GA:
                    act.activation(gel, ps, ACT.Gelu_apprx_tanh, bias=bias).then_inc(proj_taken, 1)
                else:
                    dst, o = (tma, c) if m == MA else (tmb, KC + c)
                    act.activation(dst, ps, ACT.Tanh, bias=bhalf[:, o:o + 1], scale=0.5).then_inc(proj_taken, 1)
                if j == 6:
                    act.wait_ge(gates_done, 2 * c + 2)
                    act.activation(ti, PS[:, 7, 0:T], ACT.Tanh, bias=ghalf[:, KC + c:KC + c + 1], scale=0.5)\
                       .then_inc(gates_taken, 1)
                    act.activation(tr, PS[:, 6, 0:T], ACT.Tanh, bias=ghalf[:, c:c + 1], scale=0.5)\
                       .then_inc(gates_taken, 1)
                    act.wait_ge(gates_taken, 2 * c + 4)
                    act.activation(tr, tr, ACT.Tanh, bias=sp2[:, c:c + 1], scale=sp2[:, c:c + 1]).then_inc(t_ok, 1)
                    act.wait_ge(t_ok, c + 1)
                    act.activation(sq, tr, ACT.Sqrt).then_inc(sq_ok, 1)

            for t, (t0, n) in enumerate(TILES):
                act.wait_ge(var_ok, t + 1)
                act.activation(mv[0:n, t, 3:4], mv[0:n, t, 2:3], ACT.Sqrt).then_inc(std_ok, 1)
            act.wait_ge(so_turned, 1)
            act.activation(so_rows[:, :].rearrange("r (a n) -> r a n", a=2), PS[0:54, 6:8, :], ACT.Copy)\
               .then_inc(so_ok, 1)
            act.wait_ge(so_ok, 1)
            row = 0
            for dst, n in ((h_prompt[0], 1), (h_sample[0], 8), (conv_prompt[0, 0], 3),
                           (conv_sample[0].rearrange("b j d -> (b j) d"), 24), (sc_prompt[0, 0], 2),
                           (sc_sample[0].rearrange("b j d -> (b j) d"), 16)):
                act.dma_start(dst, so_rows[row:row + n, :]).then_inc(so_out, 16)
                row += n
            for t, (t0, n) in enumerate(TILES):
                act.wait_ge(x1_turned, t + 1)
                b = (6, 0, 2)[t]
                act.activation(xT[:, :, t0:t0 + n],
                               PS[:, b:b + 2, :].rearrange("p a (k m) -> p (a k) m", m=P)[:, :, 0:n], ACT.Copy)\
                   .then_inc(x1T_ok, 1)
            act.wait_ge(top_ok, 1)
            act.activation(ek, ek, ACT.Exp).then_inc(exp_ok, 1)
            act.wait_ge(g_turned, 1)
            act.activation(gT, PS[0:NE, 6, 0:T], ACT.Copy).then_inc(gT_ok, 1)

            def take_xg(count):
                act.wait_ge(xg_done, count)
                act.activation(xg_sb, PS[:, XB, :], ACT.Copy).then_inc(xg_ok, 1)

            def take_xgT(count):
                act.wait_ge(tx_done, count)
                act.activation(xgT_f, PS[:, TB, :], ACT.Copy).then_inc(xgT_ok, 1)

            take_xg(1)
            take_xgT(1)
            act.wait_ge(items_ok, 1)
            n_pairs = act.value_load(pairs[0:1, 0:1], min_val=NE // 2, max_val=(NE + MAX_EXTRA) // 2)
            with act.Fori(0, n_pairs) as p:
                for s in range(2):
                    act.wait_ge(gm_ok, p * 2 + (s + 1))
                    act.activation(th, gm, ACT.Tanh, scale=SW_ALPHA / 2).then_inc(th_ok, 1)
                    take_xg(p * 2 + (s + 2))
                    act.wait_ge(gt_done, p * 2 + (s + 1))
                    act.activation(gt_sb[:, s, :], PS[:, TB, 0:T], ACT.Copy).then_inc(gt_ok, 1)
                    take_xgT(p * 2 + (s + 2))
                    act.wait_ge(ht_done, p * 2 + (s + 1))
                    act.activation(hT_f, PS[:, TB, :], ACT.Copy).then_inc(hT_ok, 1)
                    act.wait_ge(dn_used, p * 8 + (4 * s + 4))
                    act.activation(y_sb, PS[:, XB, :], ACT.Copy).then_inc(y_ok, 1)
            for q, t in enumerate((1, 2, 0)):
                n = TILES[t][1]
                act.wait_ge(var_ok, q + 4)
                act.activation(mv[0:n, t, 3:4], mv[0:n, t, 2:3], ACT.Sqrt).then_inc(std_ok, 1)
            act.wait_ge(so_out, 96)

        @block.tensor
        def _(pe):
            mm = pe.matmul
            pe.wait_ge(const_ok, 4)
            pe.wait_ge(x_in, 32)
            for k in range(KC):
                if k >= 6:
                    pe.wait_ge(proj_taken, k - 5)
                    pe.wait_ge(xlo_ok, k - 5)
                for t, (t0, n) in enumerate(TILES):
                    last = pe.transpose(PS[:, k % 6, t0:t0 + n], x_tok[0:n, t, k * P:(k + 1) * P], ident[0:n, 0:n])
                last.then_inc(x_turned, 1)
            pe.wait_ge(prm_in, 112)
            pe.transpose(PS[:, 6, 0:BIN], vrows[0:BIN, 0, :], ident[0:BIN, 0:BIN])
            pe.transpose(PS[:, 6, BIN:NPRM], vrows[0:7 * KC, 1, :], ident[0:7 * KC, 0:7 * KC]).then_inc(prm_turned, 1)
            pe.wait_ge(st_in, 48)
            for k in range(KC):
                last = pe.transpose(PS[:, 7, k * 48:(k + 1) * 48], st_rows[0:48, k * P:(k + 1) * P], ident[0:48, 0:48])
            last.then_inc(st_turned, 1)
            pe.wait_ge(xlo_ok, KC)

            with pe.Fori(0, KC // PB) as g:
                for q in range(7 * PB):
                    s, j = q // 7, q % 7
                    pe.wait_ge(lo_ok, g * (7 * PB) + (q + 1))
                    pe.wait_ge(proj_taken, g * (7 * PB) + (7 * s + {0: 8, 6: 9}.get(j, j + 2)))
                    for k in range(KC):
                        for n, (w, x) in enumerate(((w_hi, x_hi), (w_hi, x_lo), (w_lo, x_hi))):
                            last = mm(PS[:, j % 6, 0:T], w[:, q % RING, k, :], x[:, k, :],
                                      start=(k == 0 and n == 0), stop=(k == KC - 1 and n == 2))
                    last.then_inc(proj_done, 1)
                    if j == 6:
                        pe.wait_ge(wcur_ok, g * PB + (s + 1))
                        pe.wait_ge(xc_ok, g * PB + (s + 1))
                        pe.wait_ge(gates_taken, g * (2 * PB) + (2 * s + 2))
                        for a in range(2):
                            mm(PS[:, 6 + a, 0:T], wcur[:, a, :], xc, start=True, stop=True).then_inc(gates_done, 1)

            pe.wait_ge(proj_taken, KC + 7 * KC)
            for t, (t0, n) in enumerate(TILES):
                for k in range(KC):
                    if t == 0:
                        pe.wait_ge(block_ok, k + 2)
                        pe.wait_ge(wout_in[k // 2], 16)
                    for a in range(2):
                        last = mm(PS[0:n, 2 * t + a, :], mixT[:, k, t0:t0 + n],
                                  slot_out[:, k // 2, k % 2, a * HALF:(a + 1) * HALF],
                                  start=(k == 0), stop=(k == KC - 1))
                last.then_inc(wout_done, 1)
            pe.wait_ge(gates_taken, 2 + 2 * KC)
            for k in range(KC):
                last = pe.transpose(PS[0:54, 6 + k // 4, (k % 4) * P:(k % 4 + 1) * P], so[:, k, :], ident[:, :])
            last.then_inc(so_turned, 1)
            for t, (t0, n) in enumerate(TILES):
                pe.wait_ge(x1_ok, t + 1)
                if t == 0:
                    pe.wait_ge(so_ok, 1)
                b = (6, 0, 2)[t]
                for k in range(KC):
                    last = pe.transpose(PS[:, b + k // 4, (k % 4) * P:(k % 4) * P + n],
                                        x1[0:n, t, k * P:(k + 1) * P], ident[0:n, 0:n])
                last.then_inc(x1_turned, 1)
            pe.wait_ge(misc_in, 32)
            for t, (t0, n) in enumerate(TILES):
                pe.wait_ge(x1T_ok, t + 1)
                for k in range(KC):
                    last = mm(PS[0:n, 4, t * NE:(t + 1) * NE], xT[:, k, t0:t0 + n], rw[:, k, :],
                              start=(k == 0), stop=(k == KC - 1))
            last.then_inc(lg_done, 1)
            pe.wait_ge(mask_ok, 1)
            for t in range(4):
                terms = [(ones, u) for u in range(min(t, 3))] + ([(upper, t)] if t < 3 else [])
                for q, (m, u) in enumerate(terms):
                    last = mm(PS[:, 5, t * NE:(t + 1) * NE], m[:, :], mask[:, u, :],
                              start=(q == 0), stop=(q == len(terms) - 1))
            last.then_inc(rank_done, 1)
            pe.wait_ge(gate_ok, 1)
            for t, (t0, n) in enumerate(TILES):
                last = pe.transpose(PS[0:NE, 6, t0:t0 + n], gate[0:n, t, :], ident[0:n, 0:n])
            last.then_inc(g_turned, 1)

            def gather(count):
                pe.wait_ge(oh_ok, count)
                for t, (t0, n) in enumerate(TILES):
                    for a in range(2):
                        last = mm(PS[64 * a:64 * a + 64, XB, :], onehot[0:n, t, :],
                                  x1[0:n, t, a * HALF:(a + 1) * HALF], start=(t == 0), stop=(t == 2))
                last.then_inc(xg_done, 1)

            def turn(src, done):
                for j in range(4):
                    last = pe.transpose(PS[:, TB, j * P:(j + 1) * P], src[:, j * P:(j + 1) * P], ident[:, :])
                last.then_inc(done, 1)

            def combine(t, par):
                t0, n = TILES[t]
                for a in range(2):
                    last = mm(PS[0:n, CB[t] + a, :], gt_sb[64 * a:64 * a + 64, par, t0:t0 + n],
                              y_sb[64 * a:64 * a + 64, :], start=True, stop=True)
                last.then_inc(c_done, 1)

            gather(1)
            pe.wait_ge(xg_ok, 1)
            turn(xg_sb, tx_done)
            pe.wait_ge(items_ok, 1)
            n_pairs = pe.value_load(pairs[0:1, 0:1], min_val=NE // 2, max_val=(NE + MAX_EXTRA) // 2)
            with pe.Fori(0, n_pairs) as p:
                for s in range(2):
                    pe.wait_ge(xgT_ok, p * 2 + (s + 1))
                    if s == 0:
                        pe.wait_ge(bias_in, 32)
                    for b in range(2):
                        for a in range(2):
                            mm(PS[64 * a:64 * a + 64, b, :], esel[:, s, :],
                               bgu[:, (2 * b + a) * HALF:(2 * b + a + 1) * HALF], start=True, stop=False)
                    for k in range(KC):
                        pe.wait_ge(gu_in[gu_slot(s, k)], p * 16 + 16 if k < 2 else p * 32 + (16 * s + 16))
                        for b in range(2):
                            for a in range(2):
                                last = mm(PS[64 * a:64 * a + 64, b, :], xgT[:, k % 4, k // 4, :],
                                          ring_gu[:, gu_slot(s, k), (2 * b + a) * HALF:(2 * b + a + 1) * HALF],
                                          start=False, stop=(k == KC - 1))
                        last.then_inc(gu_used, 1)
                    pe.wait_ge(y_ok, p * 2 + (s + 1))
                    pe.wait_ge(c_taken, p * 6 + (3 * s + 3))
                    gather(p * 2 + (s + 2))
                    pe.wait_ge(cg_ok, p * 2 + (s + 1))
                    for t, (t0, n) in enumerate(TILES):
                        last = pe.transpose(PS[:, TB, t0:t0 + n], cgate[0:n, t, :, :], ident[0:n, 0:n])
                    last.then_inc(gt_done, 1)
                    combine(2, 1 - s)
                    pe.wait_ge(gt_ok, p * 2 + (s + 2))
                    pe.wait_ge(xg_ok, p * 2 + (s + 2))
                    turn(xg_sb, tx_done)
                    combine(1, 1 - s)
                    pe.wait_ge(xgT_ok, p * 2 + (s + 2))
                    pe.wait_ge(h_ok, p * 2 + (s + 1))
                    turn(up, ht_done)
                    pe.wait_ge(c_taken, p * 6 + (3 * s + 4))
                    combine(0, 1 - s)
                    pe.wait_ge(hT_ok, p * 2 + (s + 1))
                    for k in range(KC):
                        u = 4 * s + k // 2
                        if k % 2 == 0:
                            pe.wait_ge(dn_in[u], p * 16 + 16)
                        for a in range(2):
                            o = (k % 2) * D + a * HALF
                            last = mm(PS[64 * a:64 * a + 64, XB, :], hT[:, k % 4, k // 4, :],
                                      ring_dn[:, u, o:o + HALF], start=(k == 0), stop=(k == KC - 1))
                        if k % 2 == 1:
                            last.then_inc(dn_used, 1)
            pe.wait_ge(gT_ok, 1)
            pe.wait_ge(c_taken, n_pairs * 6 + 3)
            for t, b in LAST_SUMS:
                t0, n = TILES[t]
                for a in range(2):
                    mm(PS[0:n, b + a, :], gT[:, t0:t0 + n], bdn[:, a * HALF:(a + 1) * HALF], start=True, stop=False)
            pe.wait_ge(y_ok, n_pairs * 2 + 1)
            for t, b in LAST_SUMS:
                t0, n = TILES[t]
                for a in range(2):
                    last = mm(PS[0:n, b + a, :], gt_sb[64 * a:64 * a + 64, 1, t0:t0 + n],
                              y_sb[64 * a:64 * a + 64, :], start=False, stop=True)
                last.then_inc(c_done, 1)

        @block.vector
        def _(dve):
            link = Chain(dve, dve_own)
            dve.memset(xa_p[:, 0:3], 0.0).then_inc(xa_free, 1)
            link(dve.memset(cv_p[:, 0:2], 0.0))
            for k in range(KC):
                dve.wait_ge(proj_taken, k + 1)
                dve.tensor_tensor(x_lo[:, k, :], PS[:, k % 6, 0:T], x_hi[:, k, :].bitcast(F32), ALU.subtract)\
                   .then_inc(xlo_ok, 1)
            dve.wait_ge(gates_taken, 1)
            dve.tensor_scalar(bhalf, prm[:, BIN + MA * KC:BIN + (MA + 2) * KC], 0.5, None, ALU.mult)
            dve.tensor_scalar(ghalf, prm[:, LBA:LBA + 2 * KC], 0.5, None, ALU.mult)
            lam = prm[:, LAM:LAM + KC]
            ez, ab, s1, q = (spt[:, k, :] for k in range(4))
            link(dve.tensor_scalar(q, lam, -1.0, None, ALU.mult))
            dve.tensor_tensor(ab, lam, q, ALU.max).then_inc(prm_ok, 1)
            link(dve.tensor_scalar(sp2, q, 0.0, None, ALU.max))
            dve.wait_ge(prm_ok, 2)
            link(dve.tensor_scalar(s1, ez, 2.0, None, ALU.add))
            link(dve.reciprocal(q, s1))
            link(dve.tensor_tensor(s1, ez, q, ALU.mult))
            link(dve.tensor_tensor(ab, s1, s1, ALU.mult))
            link(dve.tensor_scalar(q, ab, 1.0 / 17, None, ALU.mult))
            for d in range(15, 1, -2):
                link(dve.scalar_tensor_tensor(out=q, in0=q, scalar=1.0 / d, in1=ab, op0=ALU.add, op1=ALU.mult))
            link(dve.scalar_tensor_tensor(out=q, in0=q, scalar=1.0, in1=s1, op0=ALU.add, op1=ALU.mult))
            link(dve.scalar_tensor_tensor(out=q, in0=q, scalar=2.0, in1=sp2, op0=ALU.mult, op1=ALU.add))
            dve.tensor_scalar(sp2, q, 2.0, None, ALU.mult).then_inc(prm_ok, 1)
            dve.wait_ge(gates_taken, 2)
            dve.memset(small[:, :], 0.0).then_inc(block_ok, 1)

            def par(col, c):
                return prm[:, ds(c + col, 1)]

            def stt(out, in0, scalar, in1, op0, op1):
                return dve.scalar_tensor_tensor(out=out, in0=in0, scalar=scalar, in1=in1, op0=op0, op1=op1)

            dve.wait_ge(wab_in, 64)
            with dve.Fori(0, KC) as c:
                start, off = link.n, link.off
                link.off = c * K_DENSE + off
                def taken(j):
                    dve.wait_ge(proj_taken, c * 7 + (KC + j))

                def state(lo, n):
                    return stT[:, ds(c, 1), lo:lo + n].rearrange("p a r -> p (a r)")

                def rows_of(lo, n):
                    return so[:, ds(c, 1), lo:lo + n].rearrange("p a r -> p (a r)")

                def by_seq(ap, j):
                    return ap.rearrange("p (b j) -> p b j", j=j)

                dve.tensor_copy(wcur[:, :, :], wab[:, :, ds(c, 1), :].rearrange("p a c n -> p (a c) n"))\
                   .then_inc(wcur_ok, 1)
                link(dve.tensor_copy(xa_s[:, :, 0:3], by_seq(state(8, 24), 3)))
                taken(1)
                dve.tensor_scalar(pr(xc), xa_p[:, 0:SEQ], par(CAW, c), par(CAB, c), ALU.mult, ALU.add)
                link(dve.tensor_scalar(sm(xc), xa_s[:, :, 0:DS], par(CAW, c), par(CAB, c), ALU.mult, ALU.add))
                for j in range(1, 4):
                    stt(pr(xc), xa_p[:, j:j + SEQ], par(CAW + 8 * j, c), pr(xc), ALU.mult, ALU.add)
                    last = stt(sm(xc), xa_s[:, :, j:j + DS], par(CAW + 8 * j, c), sm(xc), ALU.mult, ALU.add)
                    if j < 3:
                        link(last)
                last.then_inc(xc_ok, 1)
                dve.tensor_copy(rows_of(9, 3), xa_p[:, SEQ:SEQ + 3])
                dve.tensor_copy(by_seq(rows_of(12, 24), 3), xa_s[:, :, DS:DS + 3]).then_inc(xa_free, 1)
                dve.tensor_copy(cv_s[:, :, 0:2], by_seq(state(32, 16), 2))
                taken(3)
                dve.tensor_tensor(cv_p[:, 2:2 + SEQ], pr(cgt), pr(vt), ALU.mult)
                link(dve.tensor_tensor(cv_s[:, :, 2:2 + DS], sm(cgt), sm(vt), ALU.mult))
                dve.tensor_scalar(pr(uc), cv_p[:, 0:SEQ], par(CBW, c), None, ALU.mult)
                link(dve.tensor_scalar(sm(uc), cv_s[:, :, 0:DS], par(CBW, c), None, ALU.mult))
                for j in range(1, 3):
                    stt(pr(uc), cv_p[:, j:j + SEQ], par(CBW + 8 * j, c), pr(uc), ALU.mult, ALU.add)
                    link(stt(sm(uc), cv_s[:, :, j:j + DS], par(CBW + 8 * j, c), sm(uc), ALU.mult, ALU.add))
                dve.tensor_copy(rows_of(36, 2), cv_p[:, SEQ:SEQ + 2])
                link(dve.tensor_copy(by_seq(rows_of(38, 16), 2), cv_s[:, :, DS:DS + 2]))
                taken(7)
                link(stt(tmb, tmb, 1.0, bgt, ALU.add, ALU.mult))
                link(dve.tensor_tensor(tmb, tmb, uc, ALU.mult))
                link(stt(tma, tma, 1.0, gel, ALU.add, ALU.mult))
                dve.wait_ge(t_ok, c + 1)
                dve.wait_ge(xc_ok, c + 1)
                stt(ti, ti, 1.0, xc, ALU.add, ALU.mult)
                link(dve.tensor_scalar(aa, tr, 1.0, None, ALU.add))
                link(dve.reciprocal(rr, aa))
                dve.wait_ge(sq_ok, c + 1)
                dve.tensor_scalar(aa, rr, 2.0, -1.0, ALU.mult, ALU.add)
                link(dve.tensor_tensor(sq, sq, rr, ALU.mult))
                link(dve.tensor_tensor(ti, ti, sq, ALU.mult))
                link(dve.tensor_tensor(small[:, :], sm(aa)[:, :, 0], state(0, 8), ALU.mult))
                dve.memset(sm(aa)[:, :, 0], 0.0)
                link(dve.tensor_tensor(sm(ti)[:, :, 0], sm(ti)[:, :, 0], small[:, :], ALU.add))
                link(dve.tensor_tensor_scan(hh, aa, ti, 0.0, ALU.mult, ALU.add))
                dve.tensor_copy(rows_of(0, 1), hh[:, SEQ - 1:SEQ])
                dve.tensor_copy(rows_of(1, 8), sm(hh)[:, :, DS - 1])
                link(dve.tensor_tensor(tma, tma, hh, ALU.mult))
                dve.tensor_tensor(mixT[:, ds(c, 1), :].rearrange("p a t -> p (a t)"), tma, tmb, ALU.add)\
                   .then_inc(block_ok, 1)
                assert link.n - start == K_DENSE, link.n - start
                link.n = start
                link.off = off
            link.off = KC * K_DENSE

            def normalise(t, n, src, count, g, b):
                dve.bn_stats(stat[0:n, t, 0, :], src[0:n, t, 0:HALF])
                link(dve.bn_stats(stat[0:n, t, 1, :], src[0:n, t, HALF:D]))
                link(dve.bn_aggr(mv[0:n, t, 0:2], stat[0:n, t, :, :]))
                dve.tensor_scalar(mv[0:n, t, 2:3], mv[0:n, t, 1:2], (4 if count < 3 else 1) * EPS, None, ALU.add)\
                   .then_inc(var_ok, 1)
                dve.wait_ge(var_ok, count + 1)
                stt(x1[0:n, t, :], src[0:n, t, :], mv[0:n, t, 0:1], g[0:n, :], ALU.subtract, ALU.mult)
                dve.wait_ge(std_ok, count + 1)
                v, r, w = (mv[0:n, t, k:k + 1] for k in (2, 4, 5))
                link(dve.reciprocal(r, mv[0:n, t, 3:4]))
                link(stt(w, r, v, r, ALU.mult, ALU.mult))
                link(dve.tensor_scalar(w, w, -0.5, 1.5, ALU.mult, ALU.add))
                link(dve.tensor_tensor(r, r, w, ALU.mult))
                return stt(x1[0:n, t, :], x1[0:n, t, :], r, b[0:n, :], ALU.mult, ALU.add)

            dve.wait_ge(ln_in, 32)
            for t, (t0, n) in enumerate(TILES):
                dve.wait_ge(wout_done, t + 1)
                link(stt(x1[0:n, t, :].rearrange("p (a n) -> p a n", a=2),
                         x_tok[0:n, t, :].rearrange("p (a n) -> p a n", a=2), 2 * ALPHA,
                         PS[0:n, 2 * t:2 * t + 2, :], ALU.mult, ALU.add))
                normalise(t, n, x1, t, ln_g, ln_b).then_inc(x1_ok, 1)

            dve.wait_ge(so_out, 96)
            dve.memset(lg[:, 2, :], 0.0)
            dve.memset(tabf[0:1, :, :], 0.0)
            dve.wait_ge(lg_done, 1)
            dve.wait_ge(misc_in, 32)
            dve.wait_ge(x1_ok, 3)
            dve.tensor_tensor(lg[:, 0:2, :], PS[:, 4, 0:2 * NE].rearrange("p (t e) -> p t e", t=2),
                              rb[:, :].unsqueeze(1).to_broadcast([P, 2, NE]), ALU.add)
            link(dve.tensor_copy(small[:, 0:1], ones[:, 0:1]))
            link(dve.tensor_tensor(lg[0:NS, 2, :], PS[0:NS, 4, 2 * NE:3 * NE], rb[0:NS, :], ALU.add))
            for t in range(3):
                last = dve.max(top[:, t, :], lg[:, t, :])
            link(last)
            for t in range(3):
                last = dve.max_index(idx[:, t, :], top[:, t, :], lg[:, t, :])
            link(last)
            dve.tensor_copy(idf, idx)
            dve.tensor_tensor(ek, top[:, :, 0:TOPK], top[:, :, 0:1].to_broadcast([P, 3, TOPK]), ALU.subtract)\
               .then_inc(top_ok, 1)
            dve.wait_ge(top_ok, 1)
            for t in range(3):
                last = dve.tensor_tensor(oh4[:, t], iota[:, 0:NE].unsqueeze(1).to_broadcast([P, TOPK, NE]),
                                         idf[:, t, 0:TOPK].unsqueeze(2).to_broadcast([P, TOPK, NE]), ALU.is_equal)
            link(last)
            for t in range(3):
                last = dve.tensor_reduce(mask[:, t, :], oh4[:, t].rearrange("p k e -> p e k"), AX_X, ALU.add)
            link(last)
            dve.memset(mask[NS:P, 2, :], 0.0).then_inc(mask_ok, 1)
            dve.wait_ge(exp_ok, 1)
            link(dve.tensor_reduce(es, ek, AX_X, ALU.add))
            link(dve.reciprocal(es, es))
            link(dve.tensor_tensor(ek, ek, es.unsqueeze(2).to_broadcast([P, 3, TOPK]), ALU.mult))
            for t in range(3):
                last = dve.tensor_tensor(og4[:, t], oh4[:, t],
                                         ek[:, t, :].unsqueeze(2).to_broadcast([P, TOPK, NE]), ALU.mult)
            link(last)
            for t in range(3):
                last = dve.tensor_reduce(gate[:, t, :], og4[:, t].rearrange("p k e -> p e k"), AX_X, ALU.add)
            link(last)
            dve.memset(gate[NS:P, 2, :], 0.0).then_inc(gate_ok, 1)
            dve.wait_ge(gate_ok, 1)
            dve.tensor_scalar(gateh[:, :, :], gate[:, :, :], 0.5, None, ALU.mult)
            dve.wait_ge(rank_done, 1)
            dve.tensor_copy(cnt, PS[:, 5, 3 * NE:4 * NE])
            link(stt(posm[:, :, :], PS[:, 5, 0:3 * NE].rearrange("p (t e) -> p t e", t=3), 1.0, mask, ALU.add, ALU.mult))
            link(dve.tensor_scalar(posm[:, :, :], posm[:, :, :], -1.0, None, ALU.add))

            def pick(e, b, par):
                for t in range(3):
                    dve.tensor_scalar(onehot[:, t, :], iota[:, ds(b * ROWS, ROWS)], posm[:, t, ds(e, 1)], None, ALU.is_equal)
                dve.tensor_copy(esel[:, par, :], ident[0:NE, ds(e, 1)].to_broadcast([NE, ROWS])).then_inc(oh_ok, 1)

            def weigh(e, b):
                for t in range(3):
                    last = dve.tensor_scalar(cgate[:, t, :, :],
                                             iota[:, ds(b * ROWS, ROWS)].unsqueeze(1).to_broadcast([P, 2, ROWS]),
                                             posm[:, t, ds(e, 1)], gateh[:, t, ds(e, 1)], ALU.is_equal, ALU.mult)
                last.then_inc(cg_ok, 1)

            pick(0, 0, 0)
            weigh(0, 0)
            link(dve.tensor_scalar(ext, cnt, float(ROWS), None, ALU.is_gt))
            for b in range(2, NB):
                link(stt(ext, cnt, float(b * ROWS), ext, ALU.is_gt, ALU.add))
            link(dve.tensor_tensor_scan(incl, ones[:, 0:NE], ext, 0.0, ALU.mult, ALU.add))
            link(dve.tensor_tensor(excl, incl, ext, ALU.subtract))
            nq = 22

            def by_q(ap):
                return ap.unsqueeze(1).to_broadcast([1, nq, NE])
            qs = iota[0:1, 0:nq].unsqueeze(2).to_broadcast([1, nq, NE])
            dve.tensor_tensor(tb0, by_q(excl[0:1, :]), qs, ALU.is_le)
            link(dve.tensor_tensor(tb1, by_q(incl[0:1, :]), qs, ALU.is_gt))
            link(dve.tensor_tensor(tb0, tb0, tb1, ALU.mult))
            link(dve.tensor_tensor(tb1, tb0, by_q(iota[0:1, 0:NE]), ALU.mult))
            link(dve.tensor_reduce(tabf[0:1, 0, NE:NE + nq], tb1, AX_X, ALU.add))
            link(dve.tensor_tensor(tb1, qs, by_q(excl[0:1, :]), ALU.subtract))
            link(stt(tb1, tb1, float(1 - NB), tb0, ALU.add, ALU.mult))
            link(dve.tensor_reduce(tabf[0:1, 1, NE:NE + nq], tb1, AX_X, ALU.add))
            dve.tensor_copy(tabf[0:1, 0, 0:NE], iota[0:1, 0:NE])
            dve.tensor_scalar(prf[0:1, 0:10], iota[0:1, 0:20:2], incl[0:1, NE - 1:NE], None, ALU.is_lt)
            link(dve.tensor_scalar(tabf[0:1, 1, NE:NE + nq], tabf[0:1, 1, NE:NE + nq], float(NB), None, ALU.add))
            link(dve.tensor_reduce(prf[0:1, 10:11], prf[0:1, 0:10], AX_X, ALU.add))
            link(dve.tensor_scalar(prf[0:1, 11:12], prf[0:1, 10:11], float(NE // 2), None, ALU.add))
            dve.tensor_copy(pairs[0:1, 0:1], prf[0:1, 11:12])
            link(dve.tensor_copy(items[0:1, :, :], tabf[0:1, :, 0:64]))
            dve.memset(gt_sb[:, 1, :], 0.0).then_inc(gt_ok, 1)
            dve.memset(y_sb, 0.0).then_inc(y_ok, 1)
            dve.tensor_copy(small[:, 0:1], ones[:, 0:1]).then_inc(items_ok, 1)

            def halves(ap):
                return ap.rearrange("p (a n) -> p a n", a=2)

            def add(t, count, bank):
                n = TILES[t][1]
                dve.wait_ge(c_done, count)
                dve.tensor_tensor(halves(y_acc[0:n, t, :]), halves(y_acc[0:n, t, :]),
                                  PS[0:n, bank:bank + 2, :], ALU.add).then_inc(c_taken, 1)

            for t, (t0, n) in enumerate(TILES):
                dve.tensor_scalar(y_acc[0:n, t, :], x1[0:n, t, :], ALPHA, None, ALU.mult).then_inc(c_taken, 1)

            n_pairs = dve.value_load(pairs[0:1, 0:1], min_val=NE // 2, max_val=(NE + MAX_EXTRA) // 2)
            with dve.Fori(0, n_pairs) as p:
                start, off = link.n, link.off
                link.off = p * K_PAIR + off
                for s in range(2):
                    e = dve.value_load(items[0:1, 0, ds(p * 2 + (s + 1), 1)], min_val=0, max_val=NE - 1)
                    b = dve.value_load(items[0:1, 1, ds(p * 2 + (s + 1), 1)], min_val=0, max_val=NB)
                    dve.wait_ge(xg_done, p * 2 + (s + 1))
                    pick(e, b, 1 - s)
                    dve.wait_ge(gu_used, p * 16 + (8 * s + 8))
                    dve.tensor_scalar(gm, PS[:, 0, :], LIMIT, None, ALU.min).then_inc(gm_ok, 1)
                    link(dve.tensor_scalar(up, PS[:, 1, :], LIMIT, -LIMIT, ALU.min, ALU.max))
                    dve.wait_ge(th_ok, p * 2 + (s + 1))
                    link(stt(th, th, 1.0, gm, ALU.add, ALU.mult))
                    stt(up, up, 1.0, th, ALU.add, ALU.mult).then_inc(h_ok, 1)
                    dve.wait_ge(c_taken, p * 6 + (3 * s + 3))
                    for q, t in enumerate((2, 1, 0)):
                        add(t, p * 6 + (3 * s + q + 1), CB[t])
                    dve.wait_ge(gt_done, p * 2 + (s + 1))
                    weigh(e, b)
                assert link.n - start == K_PAIR, link.n - start
                link.n = start
                link.off = off
            dve.wait_ge(c_taken, n_pairs * 6 + 3)
            dve.wait_ge(ln2_in, 32)
            link = Chain(dve, dve_end)
            for q, t in enumerate((1, 2, 0)):
                add(t, n_pairs * 6 + (q + 1), LAST_SUMS[q][1])
                dve.wait_ge(c_taken, n_pairs * 6 + (q + 4))
                link(dve.tensor_copy(small[:, 1:2], ones[:, 0:1]))
                normalise(t, TILES[t][1], y_acc, q + 3, ln2g, ln2b).then_inc(out_ok, 1)


_INS = ["x_prompt", "x_sample", "state_rglru_h", "state_rglru_conv", "state_shortconv", "w_in", "b_in", "conv_a_w",
        "conv_a_b", "lru_wa", "lru_ba", "lru_wx", "lru_bx", "lru_lambda", "conv_b_w", "w_out", "ln1_g", "ln1_b",
        "router_w", "router_b", "w_gu", "b_gu", "w_down", "b_down", "ln2_g", "ln2_b"]
_OUTS = [(1, SEQ, D), (DB, DS, D), (1, 1, D), (1, 1, 3, D), (1, 1, 2, D), (1, DB, D), (1, DB, 3, D), (1, DB, 2, D)]


def kernel(**inputs):
    import numpy as _np
    import concourse.bacc as _bacc
    from concourse import mybir as _mybir
    from concourse.bass_utils import run_bass_kernel_spmd as _run

    nc = _bacc.Bacc("TRN2", target_bir_lowering=False, num_devices=1)
    arrays, args = {}, []
    for name in _INS:
        a = _np.ascontiguousarray(inputs[name])
        arrays[f"in_{name}"] = a
        args.append(nc.dram_tensor(f"in_{name}", a.shape, _mybir.dt.from_np(a.dtype), kind="ExternalInput").ap())
    for i, shape in enumerate(_OUTS):
        args.append(nc.dram_tensor(f"out_{i}", shape, _mybir.dt.float32, kind="ExternalOutput").ap())
    hybrid_layer(nc, *args)
    r = _run(nc, [arrays], core_ids=[0])
    return tuple(r.results[0][f"out_{i}"] for i in range(len(_OUTS)))
```

```python
from contextlib import ExitStack

import concourse.bass as bass
from concourse import mybir

P = 128
D = 1024
KC = D // P
SEQ, DB, DS = 256, 8, 8
NS = DB * DS
T = SEQ + NS
TILES = [(0, P), (P, P), (2 * P, NS)]
IN_W = 7 * D
NP = 7 * KC
RING = 4
PB = 4
OWN = 3
AHEAD = 3
NE, TOPK, FF = 32, 4, 1024
ROWS = 64
MAX_EXTRA = T * TOPK // ROWS
NB = (T + ROWS - 1) // ROWS
HALF = 512
ALPHA = 2.0 ** 0.25
EPS = 1e-5
LIMIT, SW_ALPHA = 7.0, 1.702

XA, GA, BG, CG, V, MA, MB = range(7)
ORDER = [XA, CG, V, GA, BG, MA, MB]
CAW, CAB, LBA, LBX, LAM, CBW, BIN = 0, 32, 40, 48, 56, 64, 88
NPRM = BIN + 7 * KC

ALU = mybir.AluOpType
ACT = mybir.ActivationFunctionType
AX_X = mybir.AxisListType.X
F32 = mybir.dt.float32
F32R = mybir.dt.float32r
I32 = mybir.dt.int32
U32 = mybir.dt.uint32
ds = bass.ds


XB, TB, CB = 2, 3, (4, 6, 4)
BIAS_SUMS = ((1, 6), (0, 4), (2, 2))
BIAS_AT = NE // 4
LAST_SUMS = ((1, 6), (0, 4), (2, 0))
T_ORDER = (2, 0, 1)
XT_BANK = {2: 5, 0: 0, 1: 2}
K_DENSE, K_PAIR = 20, 4


class Chain:

    def __init__(self, eng, sem):
        self.eng, self.sem, self.n, self.off = eng, sem, 0, 0

    def __call__(self, ins):
        ins.then_inc(self.sem, 1)
        self.n += 1
        self.eng.wait_ge(self.sem, self.off + self.n)


def hybrid_layer(nc, x_prompt, x_sample, state_h, state_conv, state_sc, w_in, b_in, conv_a_w,
                 conv_a_b, lru_wa, lru_ba, lru_wx, lru_bx, lru_lambda, conv_b_w, w_out, ln1_g,
                 ln1_b, router_w, router_b, w_gu, b_gu, w_down, b_down, ln2_g, ln2_b,
                 y_prompt, y_sample, h_prompt, conv_prompt, sc_prompt, h_sample, conv_sample,
                 sc_sample):
    ctx = ExitStack()
    with ctx:
        def sb(name, shape, dt=F32):
            return ctx.enter_context(nc.sbuf_tensor(name, shape, dt))

        def sem(name):
            return ctx.enter_context(nc.semaphore(name))

        base = -(-nc.sbuf_base // 32) * 32
        size = (nc.sbuf_usable_end - base) // 32 * 32
        ctx.enter_context(nc.sbuf_tensor("arena", [P, size // 4], F32))
        slot = 8 * D
        GU, DN = 0, 10 * slot
        XT, X1 = DN + 8 * slot, DN + 8 * slot + 12 * D
        MID = X1 + 12 * D
        MID_SIZE = 4 * 3776
        at = [MID + MID_SIZE + 2 * slot]

        def place(name, shape, offset, dt=F32):
            return nc.alloc_sbuf_tensor_at(name, shape, dt, offset=base + offset)

        def small_tile(name, shape, dt=F32):
            n = 4
            for d in shape[1:]:
                n *= d
            at[0] += -(-n // 32) * 32
            assert at[0] <= size, at[0] - size
            return place(name, shape, at[0] - -(-n // 32) * 32, dt)

        ring_gu = place("ring_gu", [P, 10, 2 * FF], GU)
        ring_dn = place("ring_dn", [P, 8, 2 * D], DN)

        def gu_slot(s, k):
            return KC + k if s == 1 and k < OWN else k

        ring_last = place("ring_last", [P, 2 * FF], MID + MID_SIZE + slot)

        def gu_tile(s, k):
            return ring_last[:, :] if gu_slot(s, k) == 10 else ring_gu[:, gu_slot(s, k)]

        gu_order = tuple(range(OWN, KC)) + tuple(range(OWN))

        def gu_count(s, k):
            return 8 * s + gu_order.index(k) + 1

        raw = place("raw", [P, RING, KC, P], DN)
        w_hi = place("w_hi", [P, RING, KC, P], DN + 2 * slot, F32R)
        w_lo = place("w_lo", [P, RING, KC, P], DN + 4 * slot, F32R)
        dsm = place("dsm", [P, 2 * D], DN + 7 * slot)
        dat = [0]

        def in_dsm(n):
            dat[0] += n
            assert dat[0] <= 2 * D
            return dsm[:, dat[0] - n:dat[0]]
        xa_pad, cv_pad = in_dsm(347), in_dsm(338)
        vrows = in_dsm(2 * P).rearrange("p (a n) -> p a n", a=2)
        prm = in_dsm(NPRM)
        bhalf = in_dsm(2 * KC)
        ghalf = in_dsm(2 * KC)
        sp2 = in_dsm(KC)
        spt = in_dsm(4 * KC).rearrange("p (a c) -> p a c", a=4)
        stT = in_dsm(KC * 48).rearrange("p (c r) -> p c r", c=KC)
        so = in_dsm(KC * 54).rearrange("p (c r) -> p c r", c=KC)

        x_tok = place("x_tok", [P, 3, D], XT)
        x1 = place("x1", [P, 3, D], X1)
        y_acc = x_tok
        wab = x1[:, 0:2, :].rearrange("p a (c n) -> p a c n", c=KC)
        st_rows = x1[:, 2, :]

        x_hi = place("x_hi", [P, KC, T], MID, F32R)
        x_lo = place("x_lo", [P, KC, T], MID + 10 * D, F32R)
        mixT = place("mixT", [P, KC, T], MID + 20 * D)
        xT = place("xT", [P, KC, T], MID)
        so_rows = x_tok[0:54, 0, :]
        brow = place("brow", [2 * NE, 2 * FF], MID + MID_SIZE)
        bgu, bdn, gT = brow[0:NE, :], brow[NE:2 * NE, 0:D], brow[NE:2 * NE, D:D + T]

        ident = small_tile("ident", [P, P])
        upper = small_tile("upper", [P, P])
        ones = small_tile("ones", [P, P])
        iota = small_tile("iota", [P, (NB + 1) * ROWS])
        rw = small_tile("rw", [P, KC, NE])
        rb = small_tile("rb", [P, NE])
        posm = small_tile("posm", [P, 3, NE])
        gate = small_tile("gate", [P, 3, NE])
        gateh = small_tile("gateh", [P, 3, NE])
        gt_sb = small_tile("gt_sb", [P, 2, T])
        items = small_tile("items", [1, 2, 64], I32)
        pairs = small_tile("pairs", [1, 4], I32)
        stat = small_tile("stat", [P, 3, 2, 6])
        mv = small_tile("mv", [P, 3, 8])
        small = small_tile("small", [P, 8])
        row_no = small_tile("row_no", [P, 1])

        PS = ctx.enter_context(nc.psum_tensor("PS", [P, 8, HALF], F32))

        tiles = place("tiles", [P, 12 * T + 2 * P], GU + 8 * slot)
        bgt, cgt, vt, gel, tma, tmb, xc, tr, ti, rr, aa, sq = (tiles[:, i * T:(i + 1) * T] for i in range(12))
        wcur = tiles[:, 12 * T:12 * T + 2 * P].rearrange("p (a n) -> p a n", a=2)
        hh = vt
        uc = cgt
        xa_p, xa_s = xa_pad[:, 0:259], xa_pad[:, 259:347].rearrange("p (b s) -> p b s", b=DB)
        cv_p, cv_s = cv_pad[:, 0:258], cv_pad[:, 258:338].rearrange("p (b s) -> p b s", b=DB)

        def halves(ap):
            return ap.rearrange("p (a n) -> p a n", a=2)

        def pr(t):
            return t[:, 0:SEQ]

        def sm(t):
            return t[:, SEQ:T].rearrange("p (b s) -> p b s", b=DB)

        mid = place("mid", [P, MID_SIZE // 4], MID)
        xg_sb, xgT_f, y_sb = (mid[:, i * HALF:(i + 1) * HALF] for i in range(3))
        hT_f = xg_sb
        xgT = xgT_f.rearrange("p (j a r) -> p j a r", j=4, a=2)
        hT = hT_f.rearrange("p (j a r) -> p j a r", j=4, a=2)
        onehot = mid[:, 1536:1728].rearrange("p (t r) -> p t r", t=3)
        cgate = mid[:, 1728:2112].rearrange("p (t a r) -> p t a r", t=3, a=2)
        esel = mid[0:NE, 2112:2240].rearrange("p (s r) -> p s r", s=2)
        gm, th, up = (mid[:, 2240 + i * HALF:2240 + (i + 1) * HALF] for i in range(3))
        rat = [0]

        def route(n):
            rat[0] += n
            assert rat[0] <= D
            return x_tok[:, 2, rat[0] - n:rat[0]]
        lg = route(96).rearrange("p (t e) -> p t e", t=3)
        mask = route(96).rearrange("p (t e) -> p t e", t=3)
        cnt, ext, incl, excl = (route(32) for _ in range(4))
        top = route(24).rearrange("p (t k) -> p t k", t=3)
        idx = route(24).bitcast(U32).rearrange("p (t k) -> p t k", t=3)
        idf = route(24).rearrange("p (t k) -> p t k", t=3)
        ek = route(12).rearrange("p (t k) -> p t k", t=3)
        es = route(3)
        tab = route(64).rearrange("p (a e) -> p a e", a=2)
        hit, low = route(32), route(32)
        tabc = route(2)
        prf = route(12)
        oh4 = mid[:, 2240:2624].rearrange("p (t k e) -> p t k e", t=3, k=TOPK)
        og4 = mid[:, 2624:3008].rearrange("p (t k e) -> p t k e", t=3, k=TOPK)

        x_in = sem("x_in")
        prm_in, st_in, wab_in, misc_in, ln_in = (sem(n) for n in
                                                 ("prm_in", "st_in", "wab_in", "misc_in", "ln_in"))
        raw_in = [sem(f"raw_in{j}") for j in range(RING)]
        hi_ok, lo_ok = sem("hi_ok"), sem("lo_ok")
        wout_in = [sem(f"wout_in{j}") for j in range(4)]
        bias_in = sem("bias_in")
        ln2_in = sem("ln2_in")
        gu_in = [sem(f"gu_in{k}") for k in range(KC + OWN)]
        dn_in = [sem(f"dn_in{k}") for k in range(8)]
        const_ok, zero_ok, pool_own = sem("const_ok"), sem("zero_ok"), sem("pool_own")
        x_turned, prm_turned, st_turned = sem("x_turned"), sem("prm_turned"), sem("st_turned")
        proj_done, proj_taken = sem("proj_done"), sem("proj_taken")
        gates_done, gates_taken = sem("gates_done"), sem("gates_taken")
        wcur_ok = sem("wcur_ok")
        prm_ok = sem("prm_ok")
        xa_free, cv_free, xc_ok, block_ok = sem("xa_free"), sem("cv_free"), sem("xc_ok"), sem("block_ok")
        t_ok, sq_ok = sem("t_ok"), sem("sq_ok")
        xlo_ok = sem("xlo_ok")
        wout_done, shifted = sem("wout_done"), sem("shifted")
        so_turned, so_ok = sem("so_turned"), sem("so_ok")
        var_ok, std_ok, x1_ok = sem("var_ok"), sem("std_ok"), sem("x1_ok")
        x1_turned, x1T_ok, lg_done, lg_taken = (sem(n) for n in ("x1_turned", "x1T_ok", "lg_done", "lg_taken"))
        top_ok, exp_ok = sem("top_ok"), sem("exp_ok")
        mask_ok, rank_done, gate_ok = sem("mask_ok"), sem("rank_done"), sem("gate_ok")
        g_turned, gT_ok = sem("g_turned"), sem("gT_ok")
        tab_ok, tab_done, items_ok = sem("tab_ok"), sem("tab_done"), sem("items_ok")
        oh_ok, cg_ok = sem("oh_ok"), sem("cg_ok")
        xg_done, xg_ok, tx_done, xgT_ok = (sem(n) for n in ("xg_done", "xg_ok", "tx_done", "xgT_ok"))
        gt_done, gt_ok = sem("gt_done"), sem("gt_ok")
        gu_used, dn_used = sem("gu_used"), sem("dn_used")
        gm_ok, th_ok, h_ok, ht_done, hT_ok, y_ok = (
            sem(n) for n in ("gm_ok", "th_ok", "h_ok", "ht_done", "hT_ok", "y_ok"))
        c_done, c_taken = sem("c_done"), sem("c_taken")
        bias_done, bias_taken = sem("bias_done"), sem("bias_taken")
        spread_ok, scaled_ok = sem("spread_ok"), sem("scaled_ok")
        out_ok, last_ok, out_sem, so_out = sem("out_ok"), sem("last_ok"), sem("out_sem"), sem("so_out")
        dve_own, dve_end = sem("dve_own"), sem("dve_end")

        block = ctx.enter_context(nc.Block())

        win_v = w_in[0].rearrange("(k p) n -> p k n", p=P)
        wout_v = w_out[0].rearrange("(k p) n -> p k n", p=P)
        slot_out = ring_dn[:, 0:4, :].rearrange("p j (k n) -> p j k n", k=2)
        ln_g, ln_b = ring_dn[:, 6, 0:D], ring_dn[:, 6, D:2 * D]
        ln2g, ln2b = ring_gu[:, OWN, 0:D], ring_gu[:, OWN, D:2 * D]

        @block.sync
        def _(sp):
            def load_piece(q):
                if q >= RING:
                    sp.wait_ge(lo_ok, q - RING + 1)
                col = ORDER[q % 7] * D + (q // 7) * P
                sp.dma_start(raw[:, q % RING], win_v[:, :, col:col + P]).then_inc(raw_in[q % RING], 16)

            load_piece(0)
            sp.dma_start(x_tok[:, 0:2, :], x_prompt[0].rearrange("(t p) d -> p t d", p=P)).then_inc(x_in, 16)
            sp.dma_start(x_tok[0:NS, 2, :], x_sample.rearrange("b s d -> (b s) d")).then_inc(x_in, 16)
            load_piece(1)
            rows = 0
            for src, n in ((conv_a_w, 32), (conv_a_b, 8), (lru_ba, 8), (lru_bx, 8), (lru_lambda, 8), (conv_b_w, 24)):
                v = src[0] if n > 8 else src
                sp.dma_start(vrows[rows:rows + n, 0, :], v.rearrange("a (c p) -> (a c) p", p=P)).then_inc(prm_in, 16)
                rows += n
            sp.dma_start(vrows[0:7 * KC, 1, :], b_in.rearrange("a (c p) -> (a c) p", p=P)).then_inc(prm_in, 16)
            sp.dma_start(st_rows[0:8, :], state_h[0]).then_inc(st_in, 16)
            sp.dma_start(st_rows[8:32, :], state_conv[0].rearrange("b j d -> (b j) d")).then_inc(st_in, 16)
            sp.dma_start(st_rows[32:48, :], state_sc[0].rearrange("b j d -> (b j) d")).then_inc(st_in, 16)
            for q in range(2, 4):
                load_piece(q)
            sp.wait_ge(zero_ok, 1)
            for a, w in enumerate((lru_wa, lru_wx)):
                for j in range(2):
                    sp.dma_start(wab[64 * j:64 * j + 64, a, :, 64 * j:64 * j + 64],
                                 w[0].rearrange("(c j) i o -> j i c o", j=2)[j]).then_inc(wab_in, 16)
            for q in range(4, NP):
                load_piece(q)
                if q % 4 == 3 and q < 7 + 4 * KC:
                    k = (q - 7) // 4
                    sp.dma_start(ring_gu[:, k], w_gu[0, 0, k * P:(k + 1) * P, :]).then_inc(gu_in[k], 16)
            sp.dma_start(rw[:, :, :], router_w[0].rearrange("(k p) e -> p k e", p=P)).then_inc(misc_in, 16)
            sp.dma_start(rb[:, :], router_b[0:1, :].to_broadcast([P, NE])).then_inc(misc_in, 16)
            sp.dma_start(ln_g, ln1_g[0:1, :].to_broadcast([P, D])).then_inc(ln_in, 16)
            sp.dma_start(ln_b, ln1_b[0:1, :].to_broadcast([P, D])).then_inc(ln_in, 16)
            for j in range(4):
                if j < 2:
                    sp.wait_ge(lo_ok, NP - 2 + 2 * j)
                else:
                    sp.wait_ge(proj_done, NP - 6 + 2 * j)
                sp.dma_start(slot_out[:, j], wout_v[:, 2 * j:2 * j + 2, :]).then_inc(wout_in[j], 16)

            def load_gu(e, s, k, used=None):
                src = w_gu[0, ds(e, 1), k * P:(k + 1) * P, :].rearrange("a p n -> p (a n)")
                if used is not None:
                    sp.wait_ge(gu_used, used)
                sp.dma_start(gu_tile(s, k), src).then_inc(gu_in[gu_slot(s, k)], 16)

            def load_dn(e, s, u):
                sp.dma_start(ring_dn[:, 4 * s + u, :].rearrange("p (k n) -> p k n", k=2),
                             w_down[0, ds(e, 1), 2 * u * P:(2 * u + 2) * P, :]
                             .rearrange("a (k p) n -> p (a k) n", p=P)).then_inc(dn_in[4 * s + u], 16)

            load_dn(1, 1, 0)
            load_dn(1, 1, 1)
            sp.wait_ge(block_ok, KC + 1)
            load_gu(1, 1, 0)
            load_gu(1, 1, 1)
            sp.wait_ge(wout_done, 5)
            sp.dma_start(bdn, b_down[0]).then_inc(bias_in, 16)
            sp.dma_start(bgu, b_gu[0]).then_inc(bias_in, 16)
            for u in range(4):
                load_dn(0, 0, u)
            load_gu(1, 1, 2)
            sp.wait_ge(x1_ok, 3)
            load_dn(1, 1, 2)
            sp.wait_ge(so_turned, 1)
            load_dn(1, 1, 3)
            for k in range(OWN, KC):
                load_gu(1, 1, k, gu_count(0, k))

            def load_pair(before, experts, early=False):
                for s in range(2):
                    for k in range(KC) if early and s == 0 else (0, *gu_order[:-OWN], *range(1, OWN)):
                        load_gu(experts[s], s, k, before * 16 + (16 + gu_count(0, k) if s == 1 and k >= OWN else
                                                                 gu_count(1 if k >= OWN else s, k)))
                    for u in range(4):
                        sp.wait_ge(dn_used, before * 8 + (4 * s + u + 1))
                        load_dn(experts[s], s, u)

            load_pair(0, [2, 3], early=True)
            with sp.Fori(1, NE // 2 - 1) as before:
                load_pair(before, [2 * before + 2, 2 * before + 3])
            sp.wait_ge(items_ok, 1)
            n_pairs = sp.value_load(pairs[0:1, 0:1], min_val=NE // 2, max_val=(NE + MAX_EXTRA) // 2)
            with sp.If(n_pairs > NE // 2):
                with sp.Fori(NE // 2 - 1, n_pairs - 1) as before:
                    ea = sp.value_load(items[0:1, 0, ds(2 * before + 2, 1)], min_val=0, max_val=NE - 1)
                    eb = sp.value_load(items[0:1, 0, ds(2 * before + 3, 1)], min_val=0, max_val=NE - 1)
                    load_pair(before, [ea, eb])
            sp.wait_ge(gu_used, n_pairs * 16)
            sp.dma_start(ln2g, ln2_g[0:1, :].to_broadcast([P, D])).then_inc(ln2_in, 16)
            sp.dma_start(ln2b, ln2_b[0:1, :].to_broadcast([P, D])).then_inc(ln2_in, 16)
            for q, (t, _) in enumerate(LAST_SUMS):
                t0, n = TILES[t]
                if q < 2:
                    sp.wait_ge(out_ok, q + 1)
                else:
                    sp.wait_ge(last_ok, 1)
                dst = y_prompt[0, t0:t0 + n, :] if t < 2 else y_sample.rearrange("b s d -> (b s) d")
                sp.dma_start(dst, x1[0:n, t, :]).then_inc(out_sem, 16)
            sp.wait_ge(out_sem, 48)

        @block.gpsimd
        def _(pool):
            pool.memset(ident[:, :], 0.0).then_inc(pool_own, 1)
            pool.memset(upper[:, :], 1.0).then_inc(pool_own, 1)
            pool.memset(ones[:, :], 1.0).then_inc(const_ok, 1)
            pool.wait_ge(pool_own, 2)
            pool.affine_select(out=ident[:, :], in_=ident[:, :], compare_op=ALU.not_equal, fill=1.0,
                               base=0, pattern=[[-1, P]], channel_multiplier=1).then_inc(const_ok, 1)
            pool.affine_select(out=upper[:, :], in_=upper[:, :], compare_op=ALU.is_gt, fill=0.0,
                               base=0, pattern=[[1, P]], channel_multiplier=-1).then_inc(const_ok, 1)
            pool.memset(wab, 0.0).then_inc(zero_ok, 1)
            pool.iota(iota[:, :], pattern=[[1, (NB + 1) * ROWS]], base=0, channel_multiplier=0,
                      allow_small_or_imprecise_dtypes=True).then_inc(const_ok, 1)
            pool.iota(row_no[:, :], pattern=[[0, 1]], base=0, channel_multiplier=1,
                      allow_small_or_imprecise_dtypes=True).then_inc(const_ok, 1)
            with pool.Fori(0, KC // PB) as g:
                for q in range(7 * PB):
                    pool.wait_ge(hi_ok, g * (7 * PB) + (q + 1))
                    pool.tensor_tensor(w_lo[:, q % RING], raw[:, q % RING], w_hi[:, q % RING].bitcast(F32),
                                       ALU.subtract).then_inc(lo_ok, 1)
            for q, (t, _) in enumerate(LAST_SUMS[:2]):
                n = TILES[t][1]
                pool.wait_ge(scaled_ok, q + 1)
                pool.tensor_tensor(x1[0:n, t, :], x1[0:n, t, :], ln2g[0:n, :], ALU.mult).then_inc(pool_own, 1)
                pool.wait_ge(pool_own, q + 3)
                pool.tensor_tensor(x1[0:n, t, :], x1[0:n, t, :], ln2b[0:n, :], ALU.add).then_inc(out_ok, 1)

        @block.scalar
        def _(act):
            def split_high(q):
                act.wait_ge(raw_in[q % RING], 16 * (q // RING + 1))
                if q >= RING:
                    act.wait_ge(proj_done, q - RING + 1)
                act.activation(w_hi[:, q % RING], raw[:, q % RING], ACT.Copy).then_inc(hi_ok, 1)

            split_high(0)
            for k in range(KC):
                act.wait_ge(x_turned, k + 1)
                act.activation(x_hi[:, k, :], PS[:, k % 6, 0:T], ACT.Copy).then_inc(proj_taken, 1)
            split_high(1)
            act.wait_ge(prm_turned, 1)
            act.activation(prm, PS[:, 6, 0:NPRM], ACT.Copy).then_inc(gates_taken, 1)
            act.wait_ge(st_turned, 1)
            act.activation(stT, PS[:, 7, 0:KC * 48].rearrange("p (k r) -> p k r", k=KC), ACT.Copy)\
               .then_inc(gates_taken, 1)
            split_high(2)
            act.wait_ge(prm_ok, 1)
            act.activation(spt[:, 0, :], spt[:, 1, :], ACT.Exp, scale=-1.0).then_inc(prm_ok, 1)
            act.wait_ge(prm_ok, 3)

            for q in range(NP):
                c, j = q // 7, q % 7
                m = ORDER[j]
                bias = prm[:, BIN + m * KC + c:BIN + m * KC + c + 1]
                if q + AHEAD < NP:
                    split_high(q + AHEAD)
                act.wait_ge(proj_done, q + 1)
                ps = PS[:, j % 6, 0:T]
                if m == XA:
                    act.wait_ge(xa_free, c + 1)
                    act.activation(xa_p[:, 3:259], pr(ps), ACT.Identity, bias=bias)
                    act.activation(xa_s[:, :, 3:11], sm(ps), ACT.Identity, bias=bias).then_inc(proj_taken, 1)
                elif m in (CG, V, BG):
                    if m == CG:
                        act.wait_ge(block_ok, c + 1)
                    act.activation({CG: cgt, V: vt, BG: bgt}[m], ps, ACT.Identity, bias=bias).then_inc(proj_taken, 1)
                elif m == GA:
                    act.activation(gel, ps, ACT.Gelu_apprx_tanh, bias=bias).then_inc(proj_taken, 1)
                else:
                    dst, o = (tma, c) if m == MA else (tmb, KC + c)
                    act.activation(dst, ps, ACT.Tanh, bias=bhalf[:, o:o + 1], scale=0.5).then_inc(proj_taken, 1)
                if j == 6:
                    act.wait_ge(gates_done, 2 * c + 2)
                    act.activation(ti, PS[:, 7, 0:T], ACT.Tanh, bias=ghalf[:, KC + c:KC + c + 1], scale=0.5)\
                       .then_inc(gates_taken, 1)
                    act.activation(tr, PS[:, 6, 0:T], ACT.Tanh, bias=ghalf[:, c:c + 1], scale=0.5)\
                       .then_inc(gates_taken, 1)
                    act.wait_ge(gates_taken, 2 * c + 4)
                    act.activation(tr, tr, ACT.Tanh, bias=sp2[:, c:c + 1], scale=sp2[:, c:c + 1]).then_inc(t_ok, 1)
                    act.wait_ge(t_ok, c + 1)
                    act.activation(sq, tr, ACT.Sqrt).then_inc(sq_ok, 1)

            def turned(q):
                t0, n = TILES[T_ORDER[q]]
                act.wait_ge(x1_turned, q + 1)
                b = XT_BANK[T_ORDER[q]]
                if n == P:
                    src = PS[:, b:b + 2, :].rearrange("p a (k m) -> p (a k) m", m=P)
                else:
                    src = PS[:, b, :].rearrange("p (k m) -> p k m", m=n)
                act.activation(xT[:, :, t0:t0 + n], src, ACT.Copy).then_inc(x1T_ok, 1)

            act.wait_ge(wout_done, 1)
            act.activation(x1[0:NS, 2, HALF:D], PS[64:64 + NS, 4, :], ACT.Copy).then_inc(shifted, 1)
            for q, t in enumerate(T_ORDER):
                n = TILES[t][1]
                act.wait_ge(var_ok, q + 1)
                act.activation(mv[0:n, t, 3:4], mv[0:n, t, 2:3], ACT.Sqrt).then_inc(std_ok, 1)
                if q == 1:
                    turned(0)
            turned(1)
            act.wait_ge(so_turned, 1)
            act.activation(so_rows.rearrange("r (a n) -> r a n", a=2), PS[0:54, 6:8, :], ACT.Copy)\
               .then_inc(so_ok, 1)
            turned(2)
            act.wait_ge(so_ok, 1)
            row = 0
            for dst, n in ((h_prompt[0], 1), (h_sample[0], 8), (conv_prompt[0, 0], 3),
                           (conv_sample[0].rearrange("b j d -> (b j) d"), 24), (sc_prompt[0, 0], 2),
                           (sc_sample[0].rearrange("b j d -> (b j) d"), 16)):
                act.dma_start(dst, so_rows[row:row + n, :]).then_inc(so_out, 16)
                row += n
            act.wait_ge(top_ok, 1)
            act.activation(ek, ek, ACT.Exp).then_inc(exp_ok, 1)
            act.wait_ge(g_turned, 1)
            act.activation(gT, PS[0:NE, 6, 0:T], ACT.Copy).then_inc(gT_ok, 1)

            def take_xg(count):
                act.wait_ge(xg_done, count)
                act.activation(xg_sb, PS[:, XB, :], ACT.Copy).then_inc(xg_ok, 1)

            def take_xgT(count):
                act.wait_ge(tx_done, count)
                act.activation(xgT_f, PS[:, TB, :], ACT.Copy).then_inc(xgT_ok, 1)

            take_xg(1)
            take_xgT(1)
            act.wait_ge(items_ok, 1)
            n_pairs = act.value_load(pairs[0:1, 0:1], min_val=NE // 2, max_val=(NE + MAX_EXTRA) // 2)
            with act.Fori(0, n_pairs) as p:
                for s in range(2):
                    act.wait_ge(gm_ok, p * 2 + (s + 1))
                    act.activation(th, gm, ACT.Tanh, scale=SW_ALPHA / 2).then_inc(th_ok, 1)
                    take_xg(p * 2 + (s + 2))
                    act.wait_ge(gt_done, p * 2 + (s + 1))
                    act.activation(gt_sb[:, s, :], PS[:, TB, 0:T], ACT.Copy).then_inc(gt_ok, 1)
                    take_xgT(p * 2 + (s + 2))
                    act.wait_ge(ht_done, p * 2 + (s + 1))
                    act.activation(hT_f, PS[:, TB, :], ACT.Copy).then_inc(hT_ok, 1)
                    act.wait_ge(dn_used, p * 8 + (4 * s + 4))
                    act.activation(y_sb, PS[:, XB, :], ACT.Copy).then_inc(y_ok, 1)
            for q, (t, bank) in enumerate(LAST_SUMS):
                n = TILES[t][1]
                act.wait_ge(var_ok, q + 4)
                act.activation(mv[0:n, t, 3:4], mv[0:n, t, 2:3], ACT.Sqrt).then_inc(std_ok, 1)
                if q < 2:
                    act.wait_ge(spread_ok, q + 1)
                    act.activation(halves(x1[0:n, t, :]), PS[0:n, bank:bank + 2, :], ACT.Identity, bias=mv[0:n, t, 6:7],
                                   scale=mv[0:n, t, 4:5])\
                       .then_inc(scaled_ok, 1)
            act.wait_ge(so_out, 96)

        @block.tensor
        def _(pe):
            mm = pe.matmul

            def keep_busy(n, bank):
                for _ in range(n):
                    mm(PS[:, bank, 0:P], ones[:, :], ones[:, :], start=True, stop=True)

            pe.wait_ge(const_ok, 1)
            keep_busy(24, 7)
            pe.wait_ge(const_ok, 5)
            pe.wait_ge(x_in, 32)
            for k in range(KC):
                if k >= 6:
                    pe.wait_ge(proj_taken, k - 5)
                    pe.wait_ge(xlo_ok, k - 5)
                for t, (t0, n) in enumerate(TILES):
                    last = pe.transpose(PS[:, k % 6, t0:t0 + n], x_tok[0:n, t, k * P:(k + 1) * P], ident[0:n, 0:n])
                last.then_inc(x_turned, 1)
            pe.wait_ge(prm_in, 112)
            pe.transpose(PS[:, 6, 0:BIN], vrows[0:BIN, 0, :], ident[0:BIN, 0:BIN])
            pe.transpose(PS[:, 6, BIN:NPRM], vrows[0:7 * KC, 1, :], ident[0:7 * KC, 0:7 * KC]).then_inc(prm_turned, 1)
            pe.wait_ge(st_in, 48)
            for k in range(KC):
                last = pe.transpose(PS[:, 7, k * 48:(k + 1) * 48], st_rows[0:48, k * P:(k + 1) * P], ident[0:48, 0:48])
            last.then_inc(st_turned, 1)
            pe.wait_ge(xlo_ok, KC - 1)

            with pe.Fori(0, KC // PB) as g:
                for q in range(7 * PB):
                    s, j = q // 7, q % 7
                    pe.wait_ge(lo_ok, g * (7 * PB) + (q + 1))
                    pe.wait_ge(proj_taken, g * (7 * PB) + (7 * s + {0: 8, 6: 9}.get(j, j + 2)))
                    for k in range(KC):
                        if q == 0 and k == KC - 1:
                            pe.wait_ge(xlo_ok, KC)
                        for n, (w, x) in enumerate(((w_hi, x_hi), (w_hi, x_lo), (w_lo, x_hi))):
                            last = mm(PS[:, j % 6, 0:T], w[:, q % RING, k, :], x[:, k, :],
                                      start=(k == 0 and n == 0), stop=(k == KC - 1 and n == 2))
                    last.then_inc(proj_done, 1)
                    if j == 6:
                        pe.wait_ge(wcur_ok, g * PB + (s + 1))
                        pe.wait_ge(xc_ok, g * PB + (s + 1))
                        pe.wait_ge(gates_taken, g * (2 * PB) + (2 * s + 2))
                        for a in range(2):
                            mm(PS[:, 6 + a, 0:T], wcur[:, a, :], xc, start=True, stop=True).then_inc(gates_done, 1)

            pe.wait_ge(proj_taken, KC + 7 * KC)
            def project(t, a, ks):
                t0, n = TILES[t]
                out = PS[64 * a:64 * a + n, 4, :] if t == 2 else PS[0:n, 2 * t + a, :]
                for k in ks:
                    last = mm(out, mixT[:, k, t0:t0 + n], slot_out[:, k // 2, k % 2, a * HALF:(a + 1) * HALF],
                              start=(k == 0), stop=(k == KC - 1))
                return last

            for k in range(KC - 1):
                pe.wait_ge(block_ok, k + 2)
                pe.wait_ge(wout_in[k // 2], 16)
                for a in range(2):
                    project(2, a, [k])
            project(0, 0, range(KC - 1))
            pe.wait_ge(block_ok, KC + 1)
            for a in range(2):
                last = project(2, a, [KC - 1])
            last.then_inc(wout_done, 1)
            project(0, 0, [KC - 1]).then_inc(wout_done, 1)
            for t, a in ((0, 1), (1, 0), (1, 1)):
                project(t, a, range(KC)).then_inc(wout_done, 1)

            def turn_x1(q):
                n = TILES[T_ORDER[q]][1]
                pe.wait_ge(x1_ok, q + 1)
                for k in range(KC):
                    b = XT_BANK[T_ORDER[q]] + (k * n) // HALF
                    o = (k * n) % HALF
                    last = pe.transpose(PS[:, b, o:o + n], x1[0:n, T_ORDER[q], k * P:(k + 1) * P], ident[0:n, 0:n])
                last.then_inc(x1_turned, 1)

            def logits(q):
                t = T_ORDER[q]
                t0, n = TILES[t]
                pe.wait_ge(x1T_ok, q + 1)
                for k in range(KC):
                    last = mm(PS[0:n, 4, t * NE:(t + 1) * NE], xT[:, k, t0:t0 + n], rw[:, k, :],
                              start=(k == 0), stop=(k == KC - 1))
                return last

            pe.wait_ge(misc_in, 32)
            turn_x1(0)
            turn_x1(1)
            pe.wait_ge(gates_taken, 2 + 2 * KC)
            for k in range(KC):
                last = pe.transpose(PS[0:54, 6 + k // 4, (k % 4) * P:(k % 4 + 1) * P], so[:, k, :], ident[:, :])
            last.then_inc(so_turned, 1)
            logits(0)
            logits(1)
            keep_busy(3, 1)
            turn_x1(2)
            keep_busy(2, 1)
            logits(2).then_inc(lg_done, 1)
            keep_busy(12, 1)
            pe.wait_ge(mask_ok, 1)
            for t in range(4):
                terms = [(ones, u) for u in range(min(t, 3))] + ([(upper, t)] if t < 3 else [])
                for q, (m, u) in enumerate(terms):
                    last = mm(PS[:, 5, t * NE:(t + 1) * NE], m[:, :], mask[:, u, :],
                              start=(q == 0), stop=(q == len(terms) - 1))
            last.then_inc(rank_done, 1)
            pe.wait_ge(gate_ok, 1)
            pe.wait_ge(so_ok, 1)
            for t, (t0, n) in enumerate(TILES):
                last = pe.transpose(PS[0:NE, 6, t0:t0 + n], gate[0:n, t, :], ident[0:n, 0:n])
            last.then_inc(g_turned, 1)

            def gather(count):
                pe.wait_ge(oh_ok, count)
                for t, (t0, n) in enumerate(TILES):
                    for a in range(2):
                        last = mm(PS[64 * a:64 * a + 64, XB, :], onehot[0:n, t, :],
                                  x1[0:n, t, a * HALF:(a + 1) * HALF], start=(t == 0), stop=(t == 2))
                last.then_inc(xg_done, 1)

            def turn(src, done):
                for j in range(4):
                    last = pe.transpose(PS[:, TB, j * P:(j + 1) * P], src[:, j * P:(j + 1) * P], ident[:, :])
                last.then_inc(done, 1)

            def combine(t, par):
                t0, n = TILES[t]
                for a in range(2):
                    last = mm(PS[0:n, CB[t] + a, :], gt_sb[64 * a:64 * a + 64, par, t0:t0 + n],
                              y_sb[64 * a:64 * a + 64, :], start=True, stop=True)
                last.then_inc(c_done, 1)

            def down_bias(t, b):
                t0, n = TILES[t]
                for a in range(2):
                    last = mm(PS[0:n, b + a, :], gT[:, t0:t0 + n], bdn[:, a * HALF:(a + 1) * HALF], start=True, stop=True)
                last.then_inc(bias_done, 1)

            keep_busy(6, 1)
            gather(1)
            pe.wait_ge(tab_ok, 1)
            for a in range(2):
                last = mm(PS[0:1, 5, 128 + a * NE:128 + (a + 1) * NE], tabc[:, a:a + 1], ident[:, 0:NE],
                          start=True, stop=True)
            last.then_inc(tab_done, 1)
            keep_busy(2, 1)
            pe.wait_ge(xg_ok, 1)
            turn(xg_sb, tx_done)
            keep_busy(2, 1)
            pe.wait_ge(bias_in, 32)
            def one_pair(p, biased):
                for s in range(2):
                    pe.wait_ge(xgT_ok, p * 2 + (s + 1))
                    for b in range(2):
                        for a in range(2):
                            mm(PS[64 * a:64 * a + 64, b, :], esel[:, s, :],
                               bgu[:, (2 * b + a) * HALF:(2 * b + a + 1) * HALF], start=True, stop=False)
                    for k in gu_order:
                        pe.wait_ge(gu_in[gu_slot(s, k)], p * 16 + 16 if k < OWN else p * 32 + (16 * s + 16))
                        for b in range(2):
                            for a in range(2):
                                last = mm(PS[64 * a:64 * a + 64, b, :], xgT[:, k % 4, k // 4, :],
                                          gu_tile(s, k)[:, (2 * b + a) * HALF:(2 * b + a + 1) * HALF],
                                          start=False, stop=(k == gu_order[-1]))
                        last.then_inc(gu_used, 1)
                    pe.wait_ge(y_ok, p * 2 + (s + 1))
                    pe.wait_ge(c_taken, p * 6 + (3 * s + 3))
                    if biased:
                        pe.wait_ge(bias_taken, 3)
                    gather(p * 2 + (s + 2))
                    pe.wait_ge(cg_ok, p * 2 + (s + 1))
                    for t, (t0, n) in enumerate(TILES):
                        last = pe.transpose(PS[:, TB, t0:t0 + n], cgate[0:n, t, :, :], ident[0:n, 0:n])
                    last.then_inc(gt_done, 1)
                    combine(2, 1 - s)
                    pe.wait_ge(gt_ok, p * 2 + (s + 2))
                    pe.wait_ge(xg_ok, p * 2 + (s + 2))
                    turn(xg_sb, tx_done)
                    combine(1, 1 - s)
                    pe.wait_ge(xgT_ok, p * 2 + (s + 2))
                    pe.wait_ge(h_ok, p * 2 + (s + 1))
                    turn(up, ht_done)
                    pe.wait_ge(c_taken, p * 6 + (3 * s + 4))
                    combine(0, 1 - s)
                    pe.wait_ge(hT_ok, p * 2 + (s + 1))
                    for k in range(KC):
                        u = 4 * s + k // 2
                        if k % 2 == 0:
                            pe.wait_ge(dn_in[u], p * 16 + 16)
                        for a in range(2):
                            o = (k % 2) * D + a * HALF
                            last = mm(PS[64 * a:64 * a + 64, XB, :], hT[:, k % 4, k // 4, :],
                                      ring_dn[:, u, o:o + HALF], start=(k == 0), stop=(k == KC - 1))
                        if k % 2 == 1:
                            last.then_inc(dn_used, 1)

            pe.wait_ge(gT_ok, 1)
            with pe.Fori(0, BIAS_AT) as p:
                one_pair(p, False)
            pe.wait_ge(y_ok, 2 * BIAS_AT + 1)
            pe.wait_ge(c_taken, 6 * BIAS_AT + 3)
            for t, b in BIAS_SUMS:
                down_bias(t, b)
            pe.wait_ge(items_ok, 1)
            n_pairs = pe.value_load(pairs[0:1, 0:1], min_val=NE // 2, max_val=(NE + MAX_EXTRA) // 2)
            with pe.Fori(BIAS_AT, n_pairs) as p:
                one_pair(p, True)
            pe.wait_ge(c_taken, n_pairs * 6 + 3)
            for t, b in LAST_SUMS:
                t0, n = TILES[t]
                for a in range(2):
                    mm(PS[0:n, b + a, :], ident[:, 0:n], y_acc[:, t, a * HALF:(a + 1) * HALF], start=True, stop=False)
                if (t, b) == LAST_SUMS[0]:
                    pe.wait_ge(y_ok, n_pairs * 2 + 1)
                for a in range(2):
                    last = mm(PS[0:n, b + a, :], gt_sb[64 * a:64 * a + 64, 1, t0:t0 + n],
                              y_sb[64 * a:64 * a + 64, :], start=False, stop=True)
                last.then_inc(c_done, 1)

        @block.vector
        def _(dve):
            link = Chain(dve, dve_own)
            dve.memset(xa_p[:, 0:3], 0.0).then_inc(xa_free, 1)
            link(dve.memset(cv_p[:, 0:2], 0.0))
            for k in range(KC):
                dve.wait_ge(proj_taken, k + 1)
                dve.tensor_tensor(x_lo[:, k, :], PS[:, k % 6, 0:T], x_hi[:, k, :].bitcast(F32), ALU.subtract)\
                   .then_inc(xlo_ok, 1)
            dve.wait_ge(gates_taken, 1)
            dve.tensor_scalar(bhalf, prm[:, BIN + MA * KC:BIN + (MA + 2) * KC], 0.5, None, ALU.mult)
            dve.tensor_scalar(ghalf, prm[:, LBA:LBA + 2 * KC], 0.5, None, ALU.mult)
            lam = prm[:, LAM:LAM + KC]
            ez, ab, s1, q = (spt[:, k, :] for k in range(4))
            link(dve.tensor_scalar(q, lam, -1.0, None, ALU.mult))
            dve.tensor_tensor(ab, lam, q, ALU.max).then_inc(prm_ok, 1)
            link(dve.tensor_scalar(sp2, q, 0.0, None, ALU.max))
            dve.wait_ge(prm_ok, 2)
            link(dve.tensor_scalar(s1, ez, 2.0, None, ALU.add))
            link(dve.reciprocal(q, s1))
            link(dve.tensor_tensor(s1, ez, q, ALU.mult))
            link(dve.tensor_tensor(ab, s1, s1, ALU.mult))
            link(dve.tensor_scalar(q, ab, 1.0 / 17, None, ALU.mult))
            for d in range(15, 1, -2):
                link(dve.scalar_tensor_tensor(out=q, in0=q, scalar=1.0 / d, in1=ab, op0=ALU.add, op1=ALU.mult))
            link(dve.scalar_tensor_tensor(out=q, in0=q, scalar=1.0, in1=s1, op0=ALU.add, op1=ALU.mult))
            link(dve.scalar_tensor_tensor(out=q, in0=q, scalar=2.0, in1=sp2, op0=ALU.mult, op1=ALU.add))
            dve.tensor_scalar(sp2, q, 2.0, None, ALU.mult).then_inc(prm_ok, 1)
            dve.wait_ge(gates_taken, 2)
            dve.memset(small[:, :], 0.0).then_inc(block_ok, 1)

            def par(col, c):
                return prm[:, ds(c + col, 1)]

            def stt(out, in0, scalar, in1, op0, op1):
                return dve.scalar_tensor_tensor(out=out, in0=in0, scalar=scalar, in1=in1, op0=op0, op1=op1)

            dve.wait_ge(wab_in, 64)
            with dve.Fori(0, KC) as c:
                start, off = link.n, link.off
                link.off = c * K_DENSE + off
                def taken(j):
                    dve.wait_ge(proj_taken, c * 7 + (KC + j))

                def state(lo, n):
                    return stT[:, ds(c, 1), lo:lo + n].rearrange("p a r -> p (a r)")

                def rows_of(lo, n):
                    return so[:, ds(c, 1), lo:lo + n].rearrange("p a r -> p (a r)")

                def by_seq(ap, j):
                    return ap.rearrange("p (b j) -> p b j", j=j)

                dve.tensor_copy(wcur[:, :, :], wab[:, :, ds(c, 1), :].rearrange("p a c n -> p (a c) n"))\
                   .then_inc(wcur_ok, 1)
                link(dve.tensor_copy(xa_s[:, :, 0:3], by_seq(state(8, 24), 3)))
                taken(1)
                dve.tensor_scalar(pr(xc), xa_p[:, 0:SEQ], par(CAW, c), par(CAB, c), ALU.mult, ALU.add)
                link(dve.tensor_scalar(sm(xc), xa_s[:, :, 0:DS], par(CAW, c), par(CAB, c), ALU.mult, ALU.add))
                for j in range(1, 4):
                    stt(pr(xc), xa_p[:, j:j + SEQ], par(CAW + 8 * j, c), pr(xc), ALU.mult, ALU.add)
                    last = stt(sm(xc), xa_s[:, :, j:j + DS], par(CAW + 8 * j, c), sm(xc), ALU.mult, ALU.add)
                    if j < 3:
                        link(last)
                last.then_inc(xc_ok, 1)
                dve.tensor_copy(rows_of(9, 3), xa_p[:, SEQ:SEQ + 3])
                dve.tensor_copy(by_seq(rows_of(12, 24), 3), xa_s[:, :, DS:DS + 3]).then_inc(xa_free, 1)
                dve.tensor_copy(cv_s[:, :, 0:2], by_seq(state(32, 16), 2))
                taken(3)
                dve.tensor_tensor(cv_p[:, 2:2 + SEQ], pr(cgt), pr(vt), ALU.mult)
                link(dve.tensor_tensor(cv_s[:, :, 2:2 + DS], sm(cgt), sm(vt), ALU.mult))
                dve.tensor_scalar(pr(uc), cv_p[:, 0:SEQ], par(CBW, c), None, ALU.mult)
                link(dve.tensor_scalar(sm(uc), cv_s[:, :, 0:DS], par(CBW, c), None, ALU.mult))
                for j in range(1, 3):
                    stt(pr(uc), cv_p[:, j:j + SEQ], par(CBW + 8 * j, c), pr(uc), ALU.mult, ALU.add)
                    link(stt(sm(uc), cv_s[:, :, j:j + DS], par(CBW + 8 * j, c), sm(uc), ALU.mult, ALU.add))
                dve.tensor_copy(rows_of(36, 2), cv_p[:, SEQ:SEQ + 2])
                link(dve.tensor_copy(by_seq(rows_of(38, 16), 2), cv_s[:, :, DS:DS + 2]))
                taken(7)
                link(stt(tmb, tmb, 1.0, bgt, ALU.add, ALU.mult))
                link(dve.tensor_tensor(tmb, tmb, uc, ALU.mult))
                link(stt(tma, tma, 1.0, gel, ALU.add, ALU.mult))
                dve.wait_ge(t_ok, c + 1)
                dve.wait_ge(xc_ok, c + 1)
                stt(ti, ti, 1.0, xc, ALU.add, ALU.mult)
                link(dve.tensor_scalar(aa, tr, 1.0, None, ALU.add))
                link(dve.reciprocal(rr, aa))
                dve.wait_ge(sq_ok, c + 1)
                dve.tensor_scalar(aa, rr, 2.0, -1.0, ALU.mult, ALU.add)
                link(dve.tensor_tensor(sq, sq, rr, ALU.mult))
                link(dve.tensor_tensor(ti, ti, sq, ALU.mult))
                link(dve.tensor_tensor(small[:, :], sm(aa)[:, :, 0], state(0, 8), ALU.mult))
                dve.memset(sm(aa)[:, :, 0], 0.0)
                link(dve.tensor_tensor(sm(ti)[:, :, 0], sm(ti)[:, :, 0], small[:, :], ALU.add))
                link(dve.tensor_tensor_scan(hh, aa, ti, 0.0, ALU.mult, ALU.add))
                dve.tensor_copy(rows_of(0, 1), hh[:, SEQ - 1:SEQ])
                dve.tensor_copy(rows_of(1, 8), sm(hh)[:, :, DS - 1])
                link(dve.tensor_tensor(tma, tma, hh, ALU.mult))
                dve.tensor_tensor(mixT[:, ds(c, 1), :].rearrange("p a t -> p (a t)"), tma, tmb, ALU.add)\
                   .then_inc(block_ok, 1)
                assert link.n - start == K_DENSE, link.n - start
                link.n = start
                link.off = off
            link.off = KC * K_DENSE

            def statistics(t, n, src, h):
                link(dve.bn_stats(stat[0:n, t, h, :], src[:, h, :]))

            def normalise(t, n, src, count, g, b):
                link(dve.bn_aggr(mv[0:n, t, 0:2], stat[0:n, t, :, :]))
                dve.tensor_scalar(mv[0:n, t, 2:3], mv[0:n, t, 1:2], (4 if count < 3 else 1) * EPS, None, ALU.add)\
                   .then_inc(var_ok, 1)
                dve.wait_ge(var_ok, count + 1)
                if b is not None:
                    stt(halves(x1[0:n, t, :]), src, mv[0:n, t, 0:1], halves(g[0:n, :]), ALU.subtract, ALU.mult)
                dve.wait_ge(std_ok, count + 1)
                v, r, w = (mv[0:n, t, k:k + 1] for k in (2, 4, 5))
                link(dve.reciprocal(r, mv[0:n, t, 3:4]))
                link(stt(w, r, v, r, ALU.mult, ALU.mult))
                link(dve.tensor_scalar(w, w, -0.5, 1.5, ALU.mult, ALU.add))
                link(dve.tensor_tensor(r, r, w, ALU.mult))
                if b is None:
                    return stt(mv[0:n, t, 6:7], mv[0:n, t, 0:1], -1.0, r, ALU.mult, ALU.mult)
                return stt(x1[0:n, t, :], x1[0:n, t, :], r, b[0:n, :], ALU.mult, ALU.add)

            dve.wait_ge(ln_in, 32)
            for q, t in enumerate(T_ORDER):
                n = TILES[t][1]
                for h in range(2):
                    dve.wait_ge(wout_done, 1 if t == 2 else 2 * t + 2 + h)
                    cols = slice(h * HALF, (h + 1) * HALF)
                    if t == 2 and h == 1:
                        dve.wait_ge(shifted, 1)
                        mixed = x1[0:n, t, cols]
                    else:
                        mixed = PS[0:n, 2 * t + h, :]
                    link(stt(x1[0:n, t, cols], x_tok[0:n, t, cols], 2 * ALPHA, mixed, ALU.mult, ALU.add))
                    statistics(t, n, halves(x1[0:n, t, :]), h)
                normalise(t, n, halves(x1[0:n, t, :]), q, ln_g, ln_b).then_inc(x1_ok, 1)

            dve.wait_ge(wout_done, 5)
            dve.memset(lg[:, 2, :], 0.0)
            dve.memset(items[0:1, :, :], 0.0).then_inc(zero_ok, 1)
            dve.wait_ge(zero_ok, 2)
            dve.tensor_copy(items[0:1, 0, 0:NE], iota[0:1, 0:NE])
            dve.wait_ge(lg_done, 1)
            dve.wait_ge(misc_in, 32)
            dve.wait_ge(x1_ok, 3)
            dve.tensor_tensor(lg[:, 0:2, :], PS[:, 4, 0:2 * NE].rearrange("p (t e) -> p t e", t=2),
                              rb[:, :].unsqueeze(1).to_broadcast([P, 2, NE]), ALU.add)
            link(dve.tensor_copy(small[:, 0:1], ones[:, 0:1]))
            link(dve.tensor_tensor(lg[0:NS, 2, :], PS[0:NS, 4, 2 * NE:3 * NE], rb[0:NS, :], ALU.add))
            for t in range(3):
                last = dve.max(top[:, t, :], lg[:, t, :])
            link(last)
            for t in range(3):
                last = dve.max_index(idx[:, t, :], top[:, t, :], lg[:, t, :])
            link(last)
            dve.tensor_copy(idf, idx)
            dve.tensor_tensor(ek, top[:, :, 0:TOPK], top[:, :, 0:1].to_broadcast([P, 3, TOPK]), ALU.subtract)\
               .then_inc(top_ok, 1)
            dve.wait_ge(top_ok, 1)
            for t in range(3):
                last = dve.tensor_tensor(oh4[:, t], iota[:, 0:NE].unsqueeze(1).to_broadcast([P, TOPK, NE]),
                                         idf[:, t, 0:TOPK].unsqueeze(2).to_broadcast([P, TOPK, NE]), ALU.is_equal)
            link(last)
            link(dve.tensor_reduce(mask, oh4.rearrange("p t k e -> p t e k"), AX_X, ALU.add))
            dve.memset(mask[NS:P, 2, :], 0.0).then_inc(mask_ok, 1)
            dve.wait_ge(exp_ok, 1)
            link(dve.tensor_reduce(es, ek, AX_X, ALU.add))
            link(dve.reciprocal(es, es))
            link(dve.tensor_tensor(ek, ek, es.unsqueeze(2).to_broadcast([P, 3, TOPK]), ALU.mult))
            for t in range(3):
                last = dve.tensor_tensor(og4[:, t], oh4[:, t],
                                         ek[:, t, :].unsqueeze(2).to_broadcast([P, TOPK, NE]), ALU.mult)
            link(last)
            link(dve.tensor_reduce(gate[:, :, :], og4.rearrange("p t k e -> p t e k"), AX_X, ALU.add))
            dve.memset(gate[NS:P, 2, :], 0.0).then_inc(gate_ok, 1)
            dve.wait_ge(gate_ok, 1)
            dve.tensor_scalar(gateh[:, :, :], gate[:, :, :], 0.5, None, ALU.mult)
            dve.wait_ge(rank_done, 1)
            dve.tensor_copy(cnt, PS[:, 5, 3 * NE:4 * NE])
            link(stt(posm[:, :, :], PS[:, 5, 0:3 * NE].rearrange("p (t e) -> p t e", t=3), 1.0, mask, ALU.add, ALU.mult))
            link(dve.tensor_scalar(posm[:, :, :], posm[:, :, :], -1.0, None, ALU.add))

            def pick(e, b, par):
                for t in range(3):
                    dve.tensor_scalar(onehot[:, t, :], iota[:, ds(b * ROWS, ROWS)], posm[:, t, ds(e, 1)], None, ALU.is_equal)
                dve.tensor_copy(esel[:, par, :], ident[0:NE, ds(e, 1)].to_broadcast([NE, ROWS])).then_inc(oh_ok, 1)

            def weigh(e, b):
                for t in range(3):
                    last = dve.tensor_scalar(cgate[:, t, :, :],
                                             iota[:, ds(b * ROWS, ROWS)].unsqueeze(1).to_broadcast([P, 2, ROWS]),
                                             posm[:, t, ds(e, 1)], gateh[:, t, ds(e, 1)], ALU.is_equal, ALU.mult)
                last.then_inc(cg_ok, 1)

            pick(0, 0, 0)
            link(dve.tensor_scalar(ext, cnt, float(ROWS), None, ALU.is_gt))
            for b in range(2, NB):
                link(stt(ext, cnt, float(b * ROWS), ext, ALU.is_gt, ALU.add))
            link(dve.tensor_tensor_scan(incl, ones[:, 0:NE], ext, 0.0, ALU.mult, ALU.add))
            link(dve.tensor_tensor(excl, incl, ext, ALU.subtract))
            link(dve.tensor_scalar(low, excl, row_no[:, 0:1], None, ALU.is_le))
            link(stt(hit, incl, row_no[:, 0:1], low, ALU.is_gt, ALU.mult))
            dve.tensor_tensor(tab[:, 0, :], hit, iota[:, 0:NE], ALU.mult)
            link(stt(low, excl, row_no[:, 0:1], hit, ALU.subtract, ALU.mult))
            link(stt(tab[:, 1, :], hit, float(NB - 1), low, ALU.mult, ALU.add))
            dve.tensor_reduce(tabc, tab, AX_X, ALU.add).then_inc(tab_ok, 1)
            link(dve.tensor_scalar(prf[0:1, 0:10], iota[0:1, 0:20:2], incl[0:1, NE - 1:NE], None, ALU.is_lt))
            link(dve.tensor_reduce(prf[0:1, 10:11], prf[0:1, 0:10], AX_X, ALU.add))
            dve.tensor_scalar(pairs[0:1, 0:1], prf[0:1, 10:11], float(NE // 2), None, ALU.add)
            dve.wait_ge(tab_done, 1)
            dve.tensor_copy(items[0:1, 0, NE:2 * NE], PS[0:1, 5, 128:128 + NE])
            dve.tensor_scalar(items[0:1, 1, NE:2 * NE], PS[0:1, 5, 128 + NE:128 + 2 * NE], -1.0, float(NB),
                              ALU.mult, ALU.add).then_inc(items_ok, 1)
            dve.memset(gt_sb[:, 1, :], 0.0).then_inc(gt_ok, 1)
            dve.memset(y_sb, 0.0).then_inc(y_ok, 1)
            weigh(0, 0)

            def add(t, count, bank):
                n = TILES[t][1]
                dve.wait_ge(c_done, count)
                dve.tensor_tensor(halves(y_acc[0:n, t, :]), halves(y_acc[0:n, t, :]),
                                  PS[0:n, bank:bank + 2, :], ALU.add).then_inc(c_taken, 1)

            dve.wait_ge(so_out, 96)
            dve.wait_ge(items_ok, 1)
            link(dve.memset(y_acc[NS:P, 2, :], 0.0))
            for t, (t0, n) in enumerate(TILES):
                dve.tensor_scalar(y_acc[0:n, t, :], x1[0:n, t, :], ALPHA, None, ALU.mult).then_inc(c_taken, 1)

            def one_pair(p):
                start, off = link.n, link.off
                link.off = p * K_PAIR + off
                for s in range(2):
                    e = dve.value_load(items[0:1, 0, ds(p * 2 + (s + 1), 1)], min_val=0, max_val=NE - 1)
                    b = dve.value_load(items[0:1, 1, ds(p * 2 + (s + 1), 1)], min_val=0, max_val=NB)
                    dve.wait_ge(xg_done, p * 2 + (s + 1))
                    pick(e, b, 1 - s)
                    dve.wait_ge(gu_used, p * 16 + (8 * s + 8))
                    dve.tensor_scalar(gm, PS[:, 0, :], LIMIT, None, ALU.min).then_inc(gm_ok, 1)
                    link(dve.tensor_scalar(up, PS[:, 1, :], LIMIT, -LIMIT, ALU.min, ALU.max))
                    dve.wait_ge(th_ok, p * 2 + (s + 1))
                    link(stt(th, th, 1.0, gm, ALU.add, ALU.mult))
                    stt(up, up, 1.0, th, ALU.add, ALU.mult).then_inc(h_ok, 1)
                    dve.wait_ge(c_taken, p * 6 + (3 * s + 3))
                    for q, t in enumerate((2, 1, 0)):
                        add(t, p * 6 + (3 * s + q + 1), CB[t])
                    dve.wait_ge(gt_done, p * 2 + (s + 1))
                    weigh(e, b)
                assert link.n - start == K_PAIR, link.n - start
                link.n = start
                link.off = off

            with dve.Fori(0, BIAS_AT) as p:
                one_pair(p)
            dve.wait_ge(c_taken, 6 * BIAS_AT + 3)
            for q, (t, bank) in enumerate(BIAS_SUMS):
                n = TILES[t][1]
                dve.wait_ge(bias_done, q + 1)
                dve.tensor_tensor(halves(y_acc[0:n, t, :]), halves(y_acc[0:n, t, :]),
                                  PS[0:n, bank:bank + 2, :], ALU.add).then_inc(bias_taken, 1)
            dve.wait_ge(bias_taken, 3)
            n_pairs = dve.value_load(pairs[0:1, 0:1], min_val=NE // 2, max_val=(NE + MAX_EXTRA) // 2)
            with dve.Fori(BIAS_AT, n_pairs) as p:
                one_pair(p)
            dve.wait_ge(ln2_in, 32)
            link = Chain(dve, dve_end)
            for q, (t, bank) in enumerate(LAST_SUMS):
                n = TILES[t][1]
                dve.wait_ge(c_done, n_pairs * 6 + (q + 1))
                link(dve.tensor_copy(small[:, 1:2], ones[:, 0:1]))
                y = PS[0:n, bank:bank + 2, :]
                for h in range(2):
                    statistics(t, n, y, h)
                if q < 2:
                    normalise(t, n, y, q + 3, None, None).then_inc(spread_ok, 1)
                else:
                    normalise(t, n, y, q + 3, ln2g, ln2b).then_inc(last_ok, 1)


_INS = ["x_prompt", "x_sample", "state_rglru_h", "state_rglru_conv", "state_shortconv", "w_in", "b_in", "conv_a_w",
        "conv_a_b", "lru_wa", "lru_ba", "lru_wx", "lru_bx", "lru_lambda", "conv_b_w", "w_out", "ln1_g", "ln1_b",
        "router_w", "router_b", "w_gu", "b_gu", "w_down", "b_down", "ln2_g", "ln2_b"]
_OUTS = [(1, SEQ, D), (DB, DS, D), (1, 1, D), (1, 1, 3, D), (1, 1, 2, D), (1, DB, D), (1, DB, 3, D), (1, DB, 2, D)]


def kernel(**inputs):
    import numpy as _np
    import concourse.bacc as _bacc
    from concourse import mybir as _mybir
    from concourse.bass_utils import run_bass_kernel_spmd as _run

    nc = _bacc.Bacc("TRN2", target_bir_lowering=False, num_devices=1)
    arrays, args = {}, []
    for name in _INS:
        a = _np.ascontiguousarray(inputs[name])
        arrays[f"in_{name}"] = a
        args.append(nc.dram_tensor(f"in_{name}", a.shape, _mybir.dt.from_np(a.dtype), kind="ExternalInput").ap())
    for i, shape in enumerate(_OUTS):
        args.append(nc.dram_tensor(f"out_{i}", shape, _mybir.dt.float32, kind="ExternalOutput").ap())
    hybrid_layer(nc, *args)
    r = _run(nc, [arrays], core_ids=[0])
    return tuple(r.results[0][f"out_{i}"] for i in range(len(_OUTS)))
```
